# Optimizing a Trainium2 kernel written in Bass

```python
import jax, jax.numpy as jnp
from jax import lax
import numpy as np

D_MODEL = 1024
BATCH = 1
SEQ = 512
DEPTH = 1
DEC_BATCH = 8
DEC_SEQ = 8
PAST_LEN = 2048
PAGE_SIZE = 128

R_HEAD_DIM = 64
R_HEADS = D_MODEL // (2 * R_HEAD_DIM)
R_WIDTH = R_HEADS * R_HEAD_DIM
DECAY_LORA = 64
AAA_LORA = 64
GATE_LORA = 128
LNX_EPS = 64e-5
F_HEAD_DIM = 64
F_HEADS = D_MODEL // (2 * F_HEAD_DIM)
F_WIDTH = F_HEADS * F_HEAD_DIM
Q_BLOCK = 128
N_EXPERTS = 64
TOP_K = 6
N_GROUPS = 8
TOPK_GROUPS = 4
EXPERT_FF = 256
SHARED_FF = 256
ROUTED_SCALE = 2.5
NORM_EPS = 1e-6

OFF_R = 0
OFF_K = OFF_R + R_WIDTH
OFF_V = OFF_K + R_WIDTH
OFF_WLO = OFF_V + R_WIDTH
OFF_ALO = OFF_WLO + DECAY_LORA
OFF_GLO = OFF_ALO + AAA_LORA
R_COLS = OFF_GLO + GATE_LORA
OFF_FQ = R_COLS
OFF_FK = OFF_FQ + F_WIDTH
OFF_FV = OFF_FK + F_WIDTH
OFF_FF = OFF_FV + F_WIDTH
OFF_GR = OFF_FF + F_HEADS
OFF_GF = OFF_GR + D_MODEL
IN_COLS = OFF_GF + D_MODEL

kernel_name = 'rwkv7_fox_moe_adaln_step'

F32 = jnp.float32

def rmsnorm(x, g):
    xf = x.astype(F32)
    y = xf * lax.rsqrt(jnp.mean(xf * xf, axis=-1, keepdims=True) + NORM_EPS) * g.astype(F32)
    return y.astype(x.dtype)

def modulate(x, g, shift, scale):
    return rmsnorm(x, g) * (1 + scale[:, None]) + shift[:, None]

def wkv_scan(S0, r, w, k, v, kk, a):
    def step(S, inp):
        r_t, w_t, k_t, v_t, kk_t, a_t = inp
        sa = jnp.einsum('bhij,bhj->bhi', S, -kk_t)
        S = S * w_t[:, :, None, :] + sa[..., None] * (kk_t * a_t)[:, :, None, :] + v_t[..., None] * k_t[:, :, None, :]
        return S, jnp.einsum('bhij,bhj->bhi', S, r_t)
    xs = tuple(jnp.moveaxis(t.astype(F32), 1, 0) for t in (r, w, k, v, kk, a))
    S, ys = lax.scan(step, S0.astype(F32), xs)
    return S, jnp.moveaxis(ys, 0, 1)

def rwkv7_branch(Pm, S0, p):
    B, T, _ = Pm.shape
    Pm = Pm.astype(F32)
    hs = (B, T, R_HEADS, R_HEAD_DIM)
    r = Pm[..., OFF_R:OFF_K]
    k = Pm[..., OFF_K:OFF_V]
    v = Pm[..., OFF_V:OFF_WLO]
    wlo = Pm[..., OFF_WLO:OFF_ALO]
    alo = Pm[..., OFF_ALO:OFF_GLO]
    glo = Pm[..., OFF_GLO:R_COLS]
    w_log = -jax.nn.softplus(-(p['w0'] + jnp.tanh(wlo) @ p['w_w2'])) - 0.5
    decay = jnp.exp(-jnp.exp(w_log))
    a = jax.nn.sigmoid(p['a0'] + alo @ p['w_a2'])
    g = jax.nn.sigmoid(glo) @ p['w_g2']
    kk = (k * p['k_k']).reshape(hs)
    kk = kk / jnp.maximum(jnp.linalg.norm(kk, axis=-1, keepdims=True), 1e-12)
    k = k * (1 + (a - 1) * p['k_a'])
    r, k, v, a, decay = (t.reshape(hs) for t in (r, k, v, a, decay))
    S, y = wkv_scan(S0, r, decay, k, v, kk, a)
    mu = jnp.mean(y, axis=-1, keepdims=True)
    var = jnp.mean(jnp.square(y - mu), axis=-1, keepdims=True)
    y = ((y - mu) * lax.rsqrt(var + LNX_EPS)).reshape(B, T, R_WIDTH) * p['lnx_w'] + p['lnx_b']
    bonus = jnp.sum(r * k * p['r_k'], axis=-1, keepdims=True) * v
    y = (y + bonus.reshape(B, T, R_WIDTH)) * g
    return y, S

def fox_prompt(q, k, v, logf):
    B, S, H, Dh = q.shape
    nb = S // Q_BLOCK
    scale = Dh ** -0.5
    cum = jnp.cumsum(logf, axis=1)
    cum_k = jnp.transpose(cum, (0, 2, 1))
    kpos = jnp.arange(S)
    qb = q.reshape(B, nb, Q_BLOCK, H, Dh).transpose(1, 0, 2, 3, 4)
    cb = cum.reshape(B, nb, Q_BLOCK, H).transpose(1, 0, 3, 2)
    starts = jnp.arange(nb) * Q_BLOCK

    def block(args):
        qi, ci, st = args
        s = jnp.einsum('bqhd,bkhd->bhqk', qi, k).astype(F32) * scale + ci[..., None] - cum_k[:, :, None, :]
        qpos = st + jnp.arange(Q_BLOCK)
        s = jnp.where(kpos[None, :] <= qpos[:, None], s, -jnp.inf)
        pr = jax.nn.softmax(s, axis=-1).astype(v.dtype)
        return jnp.einsum('bhqk,bkhd->bqhd', pr, v)

    o = lax.map(block, (qb, cb, starts))
    return o.transpose(1, 0, 2, 3, 4).reshape(B, S, H, Dh)

def fox_sample(q, k, v, logf, past_k, past_v, past_logf):
    B, T, H, Dh = q.shape
    P = past_k.shape[1]
    scale = Dh ** -0.5
    past_logf = past_logf.astype(F32)
    rev = jnp.sum(past_logf, axis=1, keepdims=True) - jnp.cumsum(past_logf, axis=1)
    cnew = jnp.transpose(jnp.cumsum(logf, axis=1), (0, 2, 1))
    s_past = (jnp.einsum('bqhd,bkhd->bhqk', q, past_k).astype(F32) * scale
              + cnew[..., None] + jnp.transpose(rev, (0, 2, 1))[:, :, None, :])
    s_new = jnp.einsum('bqhd,bkhd->bhqk', q, k).astype(F32) * scale + cnew[..., None] - cnew[:, :, None, :]
    tri = jnp.arange(T)[None, :] <= jnp.arange(T)[:, None]
    s_new = jnp.where(tri, s_new, -jnp.inf)
    pr = jax.nn.softmax(jnp.concatenate([s_past, s_new], axis=-1), axis=-1)
    return (jnp.einsum('bhqk,bkhd->bqhd', pr[..., :P].astype(past_v.dtype), past_v)
            + jnp.einsum('bhqk,bkhd->bqhd', pr[..., P:].astype(v.dtype), v))

def moe_ffn(h, p):
    T = h.shape[0]
    scores = jax.nn.sigmoid((h @ p['w_router']).astype(F32))
    biased = scores + p['e_bias'].astype(F32)
    grp = biased.reshape(T, N_GROUPS, N_EXPERTS // N_GROUPS)
    gscore = jnp.sum(lax.top_k(grp, 2)[0], axis=-1)
    _, gidx = lax.top_k(gscore, TOPK_GROUPS)
    gmask = jnp.sum(jax.nn.one_hot(gidx, N_GROUPS, dtype=F32), axis=1) > 0
    emask = jnp.repeat(gmask, N_EXPERTS // N_GROUPS, axis=-1)
    _, eidx = lax.top_k(jnp.where(emask, biased, -jnp.inf), TOP_K)
    wsel = jnp.take_along_axis(scores, eidx, axis=-1)
    wsel = wsel / jnp.sum(wsel, axis=-1, keepdims=True) * ROUTED_SCALE
    gate = jnp.sum(jax.nn.one_hot(eidx, N_EXPERTS, dtype=F32) * wsel[..., None], axis=1)
    hg = jnp.einsum('td,edf->tef', h, p['w_exp_gate'])
    hu = jnp.einsum('td,edf->tef', h, p['w_exp_up'])
    act = jax.nn.silu(hg) * hu * gate[..., None].astype(hg.dtype)
    routed = jnp.einsum('tef,efd->td', act, p['w_exp_down'])
    shared = (jax.nn.silu(h @ p['w_sh_gate']) * (h @ p['w_sh_up'])) @ p['w_sh_down']
    return routed + shared

def decoder_layer(x, c, shift_prev, wkv0, attend, p):
    B, T, _ = x.shape
    mod = jax.nn.silu(c) @ p['w_ada'] + p['b_ada']
    sh1, sc1, g1, sh2, sc2, g2 = jnp.split(mod, 6, axis=-1)
    h = modulate(x, p['norm1_g'], sh1, sc1)
    P = h @ p['w_in']
    Pr = P[..., :R_COLS]
    prev_proj = shift_prev @ p['w_in'][:, :R_COLS]
    Pprev = jnp.concatenate([prev_proj[:, None].astype(Pr.dtype), Pr[:, :-1]], axis=1)
    Pm = Pr + (Pprev - Pr) * p['mu_shift']
    y_r, wkv_new = rwkv7_branch(Pm, wkv0, p)
    fs = (B, T, F_HEADS, F_HEAD_DIM)
    q = P[..., OFF_FQ:OFF_FK].reshape(fs)
    k = P[..., OFF_FK:OFF_FV].reshape(fs)
    v = P[..., OFF_FV:OFF_FF].reshape(fs)
    logf = jax.nn.log_sigmoid((P[..., OFF_FF:OFF_GR] + p['b_f']).astype(F32))
    y_f = attend(q, k, v, logf).reshape(B, T, F_WIDTH)
    merged = (jax.nn.sigmoid(P[..., OFF_GR:OFF_GF]) * (y_r.astype(x.dtype) @ p['w_br_r'])
              + jax.nn.sigmoid(P[..., OFF_GF:IN_COLS]) * (y_f @ p['w_br_f']))
    x = x + g1[:, None] * (merged @ p['w_out'])
    h2 = modulate(x, p['norm2_g'], sh2, sc2)
    x = x + g2[:, None] * lax.map(lambda t: moe_ffn(t, p), h2)
    y = rmsnorm(x, p['normf_g'])
    return y, k, v, logf, wkv_new, h[:, -1]

def setup_inputs(seed: int = 0) -> dict:
    key = jax.random.key(seed)
    ks = iter(jax.random.split(key, 64))
    nrm = lambda shape, s: jax.random.normal(next(ks), shape, F32) * s
    n_pages = PAST_LEN // PAGE_SIZE
    n_used = DEC_BATCH * n_pages
    n_pool = n_used + max(1, n_used // 4)
    page_table = jax.random.permutation(next(ks), n_pool)[:n_used].reshape(DEC_BATCH, n_pages).astype(jnp.int32)
    D = D_MODEL
    return {
        'x_prompt': nrm((BATCH, SEQ, D), 1.0),
        'x_sample': nrm((DEC_BATCH, DEC_SEQ, D), 1.0),
        'c_prompt': nrm((BATCH, D), 1.0),
        'c_sample': nrm((DEC_BATCH, D), 1.0),
        'cache_k': nrm((n_pool, PAGE_SIZE, F_HEADS, F_HEAD_DIM), 1.0),
        'cache_v': nrm((n_pool, PAGE_SIZE, F_HEADS, F_HEAD_DIM), 1.0),
        'cache_logf': jax.nn.log_sigmoid(2.0 + nrm((n_pool, PAGE_SIZE, F_HEADS), 0.5)),
        'page_table': page_table,
        'state_wkv': nrm((DEC_BATCH, R_HEADS, R_HEAD_DIM, R_HEAD_DIM), 0.3),
        'state_shift': nrm((DEC_BATCH, D), 1.0),
        'w_ada': nrm((D, 6 * D), 0.5 * D ** -0.5),
        'b_ada': nrm((6 * D,), 0.02),
        'norm1_g': 1.0 + nrm((D,), 0.05),
        'w_in': nrm((D, IN_COLS), D ** -0.5),
        'mu_shift': jax.random.uniform(next(ks), (R_COLS,), F32),
        'w0': -2.0 + nrm((R_WIDTH,), 1.0),
        'w_w2': nrm((DECAY_LORA, R_WIDTH), 0.1 * DECAY_LORA ** -0.5),
        'a0': nrm((R_WIDTH,), 0.5),
        'w_a2': nrm((AAA_LORA, R_WIDTH), 0.1 * AAA_LORA ** -0.5),
        'w_g2': nrm((GATE_LORA, R_WIDTH), GATE_LORA ** -0.5),
        'k_k': 0.85 + nrm((R_WIDTH,), 0.05),
        'k_a': 1.0 + nrm((R_WIDTH,), 0.05),
        'r_k': nrm((R_HEADS, R_HEAD_DIM), 0.1),
        'lnx_w': 1.0 + nrm((R_WIDTH,), 0.05),
        'lnx_b': nrm((R_WIDTH,), 0.02),
        'b_f': 2.0 + nrm((F_HEADS,), 0.5),
        'w_br_r': nrm((R_WIDTH, D), R_WIDTH ** -0.5),
        'w_br_f': nrm((F_WIDTH, D), F_WIDTH ** -0.5),
        'w_out': nrm((D, D), D ** -0.5),
        'norm2_g': 1.0 + nrm((D,), 0.05),
        'w_router': nrm((D, N_EXPERTS), D ** -0.5),
        'e_bias': nrm((N_EXPERTS,), 0.01),
        'w_exp_gate': nrm((N_EXPERTS, D, EXPERT_FF), D ** -0.5),
        'w_exp_up': nrm((N_EXPERTS, D, EXPERT_FF), D ** -0.5),
        'w_exp_down': nrm((N_EXPERTS, EXPERT_FF, D), EXPERT_FF ** -0.5),
        'w_sh_gate': nrm((D, SHARED_FF), D ** -0.5),
        'w_sh_up': nrm((D, SHARED_FF), D ** -0.5),
        'w_sh_down': nrm((SHARED_FF, D), SHARED_FF ** -0.5),
        'normf_g': 1.0 + nrm((D,), 0.05),
    }

def reference(x_prompt, x_sample, c_prompt, c_sample, cache_k, cache_v, cache_logf, page_table,
              state_wkv, state_shift, w_ada, b_ada, norm1_g, w_in, mu_shift, w0, w_w2, a0, w_a2, w_g2,
              k_k, k_a, r_k, lnx_w, lnx_b, b_f, w_br_r, w_br_f, w_out, norm2_g, w_router, e_bias,
              w_exp_gate, w_exp_up, w_exp_down, w_sh_gate, w_sh_up, w_sh_down, normf_g):
    p = dict(w_ada=w_ada, b_ada=b_ada, norm1_g=norm1_g, w_in=w_in, mu_shift=mu_shift, w0=w0, w_w2=w_w2,
             a0=a0, w_a2=w_a2, w_g2=w_g2, k_k=k_k, k_a=k_a, r_k=r_k, lnx_w=lnx_w, lnx_b=lnx_b, b_f=b_f,
             w_br_r=w_br_r, w_br_f=w_br_f, w_out=w_out, norm2_g=norm2_g, w_router=w_router, e_bias=e_bias,
             w_exp_gate=w_exp_gate, w_exp_up=w_exp_up, w_exp_down=w_exp_down, w_sh_gate=w_sh_gate,
             w_sh_up=w_sh_up, w_sh_down=w_sh_down, normf_g=normf_g)
    B = x_prompt.shape[0]
    for _ in range(DEPTH):
        yp, kp, vp, lfp, wkvp, shp = decoder_layer(
            x_prompt, c_prompt, jnp.zeros((B, D_MODEL), x_prompt.dtype),
            jnp.zeros((B, R_HEADS, R_HEAD_DIM, R_HEAD_DIM), F32), fox_prompt, p)
    nb, npg = page_table.shape
    past_k = cache_k[page_table].reshape(nb, npg * PAGE_SIZE, F_HEADS, F_HEAD_DIM)
    past_v = cache_v[page_table].reshape(nb, npg * PAGE_SIZE, F_HEADS, F_HEAD_DIM)
    past_lf = cache_logf[page_table].reshape(nb, npg * PAGE_SIZE, F_HEADS)
    attend_s = lambda q, k, v, lf: fox_sample(q, k, v, lf, past_k, past_v, past_lf)
    for _ in range(DEPTH):
        ys, ks_, vs, lfs, wkvs, shs = decoder_layer(x_sample, c_sample, state_shift, state_wkv, attend_s, p)
    return (yp, ys, kp, vp, lfp, wkvp, shp, ks_, vs, lfs, wkvs, shs)


_drawn_inputs = setup_inputs


def setup_inputs(seed=0):
    import zlib

    import numpy as np

    out = dict(_drawn_inputs(seed))
    spreads = {}
    factors = {'cache_logf': 20.775, 'w_w2': 4.204, 'lnx_w': 2.944, 'lnx_b': 7.287}
    for name, (base, spread) in spreads.items():
        noise = np.random.default_rng([zlib.crc32(name.encode()), seed]).standard_normal(out[name].shape)
        drawn = base * np.exp(spread * noise) if base else spread * noise
        out[name] = __import__('jax').numpy.asarray(drawn.astype(out[name].dtype))
    for name, factor in factors.items():
        out[name] = (out[name] * factor).astype(out[name].dtype)
    return out
```

```python
from contextlib import ExitStack

import numpy as np

import concourse.bass as bass
from concourse import mybir

ALU = mybir.AluOpType
ACT = mybir.ActivationFunctionType
AX = mybir.AxisListType
F32 = mybir.dt.float32
I32 = mybir.dt.int32
U32 = mybir.dt.uint32

D = 1024
DC = D // 128
NP_ = 512
NB = 8
NS = 8
NSM = NB * NS
NT = NP_ + NSM
NTP = NP_ // 128
NTT = NTP + 1
H = 8
HD = 64
W = H * HD
NPAIR = H // 2
RC = 3 * W + 256
RCH = RC // 128
OFQ, OFK, OFV, OFF_, OGR, OGF = RC, RC + W, RC + 2 * W, RC + 3 * W, RC + 3 * W + H, RC + 3 * W + H + D
NCOL = NT + NB
NPG = 16
PG = 128
PAST = NPG * PG
NE = 64
TOPK = 6
EFF = 256
ROUTED_SCALE = 2.5
EPS = 1e-6
LNX_EPS = 64e-5
DECAY_MAX = float(np.exp(-0.5))
MAXI = NE + (NT * TOPK) // 128 + 3
NOWHERE = 100000
BIG = 1e30

INS = ['x_prompt', 'x_sample', 'c_prompt', 'c_sample', 'cache_k', 'cache_v', 'cache_logf', 'page_table',
       'state_wkv', 'state_shift', 'w_ada', 'b_ada', 'norm1_g', 'w_in', 'mu_shift', 'w0', 'w_w2', 'a0', 'w_a2',
       'w_g2', 'k_k', 'k_a', 'r_k', 'lnx_w', 'lnx_b', 'b_f', 'w_br_r', 'w_br_f', 'w_out', 'norm2_g', 'w_router',
       'e_bias', 'w_exp_gate', 'w_exp_up', 'w_exp_down', 'w_sh_gate', 'w_sh_up', 'w_sh_down', 'normf_g']
OUTS = [('y_prompt', (1, NP_, D)), ('y_sample', (NB, NS, D)), ('k_prompt', (1, NP_, H, HD)),
        ('v_prompt', (1, NP_, H, HD)), ('logf_prompt', (1, NP_, H)), ('wkv_prompt', (1, H, HD, HD)),
        ('shift_prompt', (1, D)), ('k_sample', (NB, NS, H, HD)), ('v_sample', (NB, NS, H, HD)),
        ('logf_sample', (NB, NS, H)), ('wkv_sample', (NB, H, HD, HD)), ('shift_sample', (NB, D))]


def tile_rows(i):
    return 128 if i < NTP else NSM


def build(nc, t, o):
    ctx = ExitStack()
    with ctx:
        ARENA = 53100
        arena = ctx.enter_context(nc.sbuf_tensor("arena", [128, ARENA], F32))
        psum = ctx.enter_context(nc.psum_tensor("psum", [128, 8, 512], F32))

        def view(off, *dims):
            n = int(np.prod(dims))
            assert off + n <= ARENA, (off, dims)
            a = arena[:, off:off + n]
            if len(dims) == 2:
                a = a.rearrange("p (a b) -> p a b", a=dims[0])
            elif len(dims) == 3:
                a = a.rearrange("p (a b c) -> p a b c", a=dims[0], b=dims[1])
            return a

        at = [0]

        def take(*dims):
            a = view(at[0], *dims)
            at[0] += int(np.prod(dims))
            return a

        def sem(name):
            return ctx.enter_context(nc.semaphore(name))

        def scratch(name, shape, dt=F32):
            return nc.dram_tensor(name, shape, dt).ap()

        ident, ones = take(128), take(128)
        up_incl, up_strict, low_neg, blk64 = take(128), take(128), take(128), take(128)
        same = take(8, 128)
        level = take(7, 128)
        mask_p, mask_s = take(4, 128), take(4, 128)
        segment = take(NT)
        head_rows = take(NB, H, NS)
        head8 = take(H, NS)
        neg_new = take(NB, NSM)
        tri8 = take(NS)
        lower16 = take(128)
        PAR = take(64)
        mu_c = take(RCH)
        w0c, w0n, a0c, kkc, kac, ka1, rkc, lwc, lbc = [take(NPAIR) for _ in range(9)]
        bf_c, eps1, epsx = take(1), take(1), take(1)
        ss, rstd = take(8), take(8)
        e_mid, e_end = take(NPAIR, NTP), take(NPAIR, NTP)
        e_end_s = take(NPAIR, NB)
        c_mid = take(NPAIR, NTP)
        cum, fabs, lf_tmp = take(NT), take(NT), take(64)
        small_at = [at[0]]
        at[0] += 40
        CONST = at[0]

        def take_small(n):
            small_at[0] += n
            assert small_at[0] <= CONST
            return view(small_at[0] - n, n)

        hT = take(DC, NCOL)
        PM = take(RCH, NT)
        qT, kT, vtok = take(NPAIR, NT), take(NPAIR, NT), take(NTT, W)
        ring0 = at[0]
        wring = [take(DC, 512) for _ in range(3)]
        small0 = at[0]
        KK, AA, LW, CC, GG, BV = [take(NPAIR, NT) for _ in range(6)]
        end0 = at[0]
        x_all = view(small0, NTT, D)
        bcast = view(small0 + NTT * D, 2, 2, D)
        PM0 = CONST + DC * NCOL
        mod = view(PM0, 6 * D)
        gains = view(small0 + 11600, 2, D)[0:NB + 1]
        QKV0 = PM0 + RCH * NT
        bada = view(QKV0, 6 * D)[0:NB + 1]
        cT = view(QKV0 + 6 * D, NB + 1, DC)
        cE = view(QKV0 + 6 * D + 80, NB + 1, DC)
        sqjunk = view(small0 + 4 * 2304, D)
        raw = [view(small0 + 4 * 2304 + k * 600, 1 + NP_ + NB * (NS + 1)) for k in range(2)]
        sstate = view(small0 + 4 * 2304 + 1300, D)[0:NB]
        slot2 = ring0 + 2 * DC * 512
        fT = view(slot2 + 2600, NT)
        ktok = view(slot2, NTT, W)
        lftok = view(slot2 + 2560, NTT, H)
        lora_wa, lora_g = view(small0 + 5 * 2304, W), view(small0 + 5 * 2304 + W, W)
        exp_neg = [view(ring0 + 600 * k, NT) for k in range(2)]
        Rb, Ub = view(ring0, H, HD), view(ring0 + 512, H, HD)
        Sst, S0 = view(ring0 + 1024, NPAIR, HD), view(ring0 + 1280, NPAIR, HD)
        TM = view(ring0 + 1536, NPAIR, 3, 128)
        AT0 = ring0 + 1536 + 1536
        AT = view(AT0, H, 4 * 128)
        TI0 = AT0 + 4096
        TI = [view(TI0 + h * 256, 2, 128) for h in range(H)]
        TIg = [view(TI0 + g * 1024, 4, 2, 128) for g in range(2)]
        TP = [view(TI0 + 2048 + g * 512, 4, 128) for g in range(2)]
        ML = [view(TI0 + 3072 + g * 512, 4, 128) for g in range(2)]
        assert TI0 + 4096 <= small0
        ro_sb = view(TI0 + 2048, 2, 256)
        prompt_state = view(TI0 + 3072, 512)[0:HD]
        YT = LW
        Pb, PTb = [view(small0 + 5 * 2304 + 512 * k, 512) for k in range(2)], [view(small0 + 5 * 2304 + 1024 + 512 * k, 512) for k in range(2)]
        lf_pages, rev = view(small0 + 4 * 2304, PG, H), view(small0 + 4 * 2304 + 1024, H, PG)
        yfT = CC
        kpage = [view(ring0 + 2048 * k, 4, W) for k in range(2)]
        vpage = [view(ring0 + 4096 + 2048 * k, 4, W) for k in range(2)]
        revT = view(ring0 + 8192, PAST)[0:64]
        qblk = view(ring0 + 8192 + 2048, NB * NPAIR * 64)
        Ssb = [view(PM0 + k * (PAST + 64), PAST + 64)[0:64] for k in range(2)]
        PTs = [view(PM0 + 2 * (PAST + 64) + k * 17 * 64, 17, 64) for k in range(2)]
        KTb = [view(PM0 + 2 * (PAST + 64) + 34 * 64 + k * 512, 512) for k in range(2)]
        Osb = view(small0 + 4 * 2304, W)[0:64]
        row_sum, nmx = take_small(2), take_small(2)
        page_ids = take_small(1).bitcast(I32)
        sum_off = take_small(2 * H)
        row_inv = take_small(2)
        revD = scratch("revD", (NB, H, NPG, PG))
        mergedT = view(small0, DC, NT)
        w_brr = view(PM0, NPAIR, D)
        sg = [view(PM0 + 4096 + k * NT, NT) for k in range(2)]
        mt2 = view(PM0 + 4096 + 2 * NT, NT)
        w_brf = view(small0 + 4 * 2304, NPAIR, D)
        x1 = view(QKV0, NTT, D)
        bc2 = view(PM0, 3, 2, D)
        h2 = view(small0 + 2 * 2304, NTT, D)
        h2D = scratch("h2D", (NT, D))
        xo_tmp = view(small0 + 3 * 2304 - 0, 512)
        junk2 = view(small0, D)
        act_s = [view(small0 + 1024 + 256 * k, EFF) for k in range(2)]
        actT_s = [view(small0 + 1536 + 256 * k, 2, 128) for k in range(2)]
        sil_s = [view(small0 + 2048 + 256 * k, EFF) for k in range(2)]
        rt = [PM0]

        def route(*dims):
            a = view(rt[0], *dims)
            rt[0] += int(np.prod(dims))
            assert rt[0] <= PM0 + RCH * NT
            return a

        score, biased, masked = route(NTT, NE), route(NTT, NE), route(NTT, NE)
        top8, gtop, gscore, gmask, gpen = route(NTT, 8, 8), route(NTT, 8), route(NTT, 8), route(NTT, 8), route(NTT, 8)
        gidx_u, gidx = route(NTT * 8).bitcast(U32).rearrange("p (a b) -> p a b", a=NTT), route(NTT, 8)
        geq = route(NTT, 8, 4)
        etop, eidx_u, eidx = route(NTT, 8), route(NTT * 8).bitcast(U32).rearrange("p (a b) -> p a b", a=NTT), route(NTT, 8)
        onehot, prod = route(NTT, TOPK, NE), route(NTT, TOPK, NE)
        chosen, rank, over = route(NTT, NE), route(NTT, NE), route(NTT, NE)
        count, ntile, tile_end, tile_start, cmp_i = route(NE), route(NE), route(NE), route(NE), route(NE)
        wsum, valid, iota64, ebias = route(8), route(8), route(NE), route(NE)
        posf = route(NTT, TOPK)
        item_f, item_i, n_i, iota_p = route(1), route(1).bitcast(I32), route(1).bitcast(I32), route(1)
        fill = route(2 * MAXI).bitcast(I32)
        keep = small0 + 3000
        wsel = view(keep, NTT, TOPK)
        pos_i = view(keep + 30, NTT * TOPK).bitcast(I32)
        payload = view(keep + 60, NTT * TOPK * 2).bitcast(I32)
        slots = view(keep + 120, 2 * MAXI).bitcast(I32)
        g_idx, s_idx = [view(keep + 320 + 2 * k, 1).bitcast(I32) for k in range(2)], [view(keep + 324 + 2 * k, 1).bitcast(I32) for k in range(2)]
        slotD = scratch("slotD", (128 * MAXI, 2), I32)
        itemD = scratch("itemD", (1, 136), I32)
        ykD = scratch("ykD", (NT * TOPK, D))
        hg = [view(CONST + 1024 * k, D) for k in range(2)]
        hgT = [view(CONST + 2048 + 1024 * k, DC, 128) for k in range(2)]
        wgu = [view(ring0 + 6144 * k, 2, DC, EFF) for k in range(2)]
        wdn = [view(ring0 + 6144 * k + 4096, 2, D) for k in range(2)]
        ye = [view(PM0 + 1024 * k, D) for k in range(2)]
        sile, acte, acteT = [[view(PM0 + 2048 + 256 * (2 * j + k), 256) for k in range(2)] for j in range(3)]
        acteT = [a.rearrange("p (c s) -> p c s", c=2) for a in acteT]
        ykb = [view(ring0 + 6144 * k, TOPK, D) for k in range(2)]
        g2b, nfb = view(small0 + 9728, 2, D), view(small0 + 9728 + 2048, D)
        rho, khat, vT = PM[:, 0:NPAIR], PM[:, NPAIR:2 * NPAIR], PM[:, 2 * NPAIR:3 * NPAIR]
        modD = scratch("modD", (NB + 1, 6 * D))

        blocks = [("ada", j) for j in range(12)] + [("in", j) for j in range(8)] + [
            ("gate", OGR), ("gate", OGF), ("gate", OGR + 512), ("gate", OGF + 512), ("out", 0), ("out", 1), ("shared", 0), ("down", 0)]
        in_cols = [(0, 512), (512, 1024), (1024, 1536), (1536, RC), (OFQ, OFK), (OFK, OFV), (OFV, OFF_), (OFF_, OGR)]

        def block_used(n):
            if n < 12:
                return ada_ps, n + 1
            if n < 18:
                return pj_ps, sum((b - a) // 128 for a, b in in_cols[:n - 11])
            if n < 20:
                return v_ps, NTT + n - 18
            if n < 24:
                return mg_ps, 16 * ((n - 20) // 2) + 15 + (n - 20) % 2
            if n < 26:
                return xo_ps, NTT * (n - 23)
            return sg_ps, NTT

        w_landed = [sem(f"w_landed{k}") for k in range(3)]
        c_landed, b_landed, g_landed, x_landed, par_landed = sem("c_landed"), sem("b_landed"), sem("g_landed"), sem("x_landed"), sem("par_landed")
        pool_const, dve_const = sem("pool_const"), sem("dve_const")
        c_exp, c_ready = sem("c_exp"), sem("c_ready")
        ada_ps, ada_out = sem("ada_ps"), sem("ada_out")
        mod_stored, bc_landed = sem("mod_stored"), sem("bc_landed")
        sq1, ms1, sqrt1, h_ready = sem("sq1"), sem("ms1"), sem("sqrt1"), sem("h_ready")
        tr1, ev1 = sem("tr1"), sem("ev1")
        pj_ps, pj_out = sem("pj_ps"), sem("pj_out")
        mixed = sem("mixed")
        v_ps, v_out, f_act, lf_done = sem("v_ps"), sem("v_out"), sem("f_act"), sem("lf_done")
        shift_out = sem("shift_out")
        kt_ps, kt_out, lf_ps, lf_out = sem("kt_ps"), sem("kt_out"), sem("lf_ps"), sem("lf_out")
        out_sem = sem("out_sem")
        order_dve, order_act, order_pool = sem("order_dve"), sem("order_act"), sem("order_pool")
        lora_landed, lora_in, lora_ps, lora_out = sem("lora_landed"), sem("lora_in"), sem("lora_ps"), sem("lora_out")
        kk_raw, kk_sq, kk_n2, kk_norm = sem("kk_raw"), sem("kk_sq"), sem("kk_n2"), sem("kk_norm")
        e_neg, r_out_s = sem("e_neg"), sem("r_out_s")
        rk_in, rk_ps, t1_ready, e_ready, prep_done = sem("rk_in"), sem("rk_ps"), sem("t1_ready"), sem("e_ready"), sem("prep_done")
        kv_stored = sem("kv_stored")
        tm_ps, tm_out, at_ps, at_out = sem("tm_ps"), sem("tm_out"), sem("at_ps"), sem("at_out")
        ml_done, p_ps, p_out, dt_ps, t_add = sem("ml_done"), sem("p_ps"), sem("p_out"), sem("dt_ps"), sem("t_add")
        s0_ready, r_ps, r_out, u_ps, u_out = sem("s0_ready"), sem("r_ps"), sem("r_out"), sem("u_ps"), sem("u_out")
        y_ps, y_out, s_ps, s_out = sem("y_ps"), sem("y_out"), sem("s_ps"), sem("s_out")
        st_ps, st_out = sem("st_ps"), sem("st_out")
        ro_ps, ro_out = sem("ro_ps"), sem("ro_out")
        x_ready, x_ps, x_out, w_ps, w_out_ = sem("x_ready"), sem("x_ps"), sem("x_out"), sem("w_ps"), sem("w_out_")
        ln_in, ln_mu, ln_sq, ln_var, ln_sd, yr_done = sem("ln_in"), sem("ln_mu"), sem("ln_sq"), sem("ln_var"), sem("ln_sd"), sem("yr_done")

        at_sc, at_mx, at_ex, at_pn = sem("at_sc"), sem("at_mx"), sem("at_ex"), sem("at_pn")
        at_tp, at_pt, at_o, at_oe = sem("at_tp"), sem("at_pt"), sem("at_o"), sem("at_oe")
        pg_ids, lf_landed, rev_ps = sem("pg_ids"), sem("lf_landed"), sem("rev_ps")
        rev_stored, rev_landed = sem("rev_stored"), sem("rev_landed")
        k_landed, v_landed = [sem(f"k_landed{k}") for k in range(2)], [sem(f"v_landed{k}") for k in range(2)]
        kt_tr, kq_mm, kte = sem("kt_tr"), sem("kq_mm"), [sem(f"kte{k}") for k in range(2)]
        sc_out, nw_ps, nw_out = sem("sc_out"), sem("nw_ps"), sem("nw_out")
        vq_mm, ot_ps, yf_out = sem("vq_mm"), sem("ot_ps"), sem("yf_out")
        br_landed, mg_ps, mg_sg, mg_out = sem("br_landed"), sem("mg_ps"), sem("mg_sg"), sem("mg_out")
        xo_ps, x1_done = sem("xo_ps"), sem("x1_done")
        sg_ps, sg_act, sg_mul, sg_tr, sg_at, sd_ps, sd_out = sem("sg_ps"), sem("sg_act"), sem("sg_mul"), sem("sg_tr"), sem("sg_at"), sem("sd_ps"), sem("sd_out")

        lg_ps, chosen_done, slots_in, tables, slot_filled = sem("lg_ps"), sem("chosen_done"), sem("slots_in"), sem("tables"), sem("slot_filled")
        eb_landed, slot_set, slots_landed, items_stored, pool_route = sem("eb_landed"), sem("slot_set"), sem("slots_landed"), sem("items_stored"), sem("pool_route")
        hg_landed = [sem(f"hg_landed{k}") for k in range(2)]
        gu_landed, dn_landed = [sem(f"gu_landed{k}") for k in range(2)], [sem(f"dn_landed{k}") for k in range(2)]
        hx_v = sem("hx_v")
        y_a = sem("y_a")
        y_stored, idx_g, idx_s = [sem(f"y_stored{k}") for k in range(2)], sem("idx_g"), sem("idx_s")
        yk_landed = [sem(f"yk_landed{k}") for k in range(2)]

        def n_items(eng):
            eng.wait_ge(items_stored, 32)
            return eng.value_load(itemD[0:1, 128:129], min_val=24, max_val=(NT * TOPK + 127 * NE) // 128 - 4)

        def levels(i):
            return 7 if i < NTP else 3

        def lv(i, m, g):
            return 14 * i + 2 * m + g + 1

        def lvp(i, m, g):
            return 12 * i + 2 * (m - 1) + g + 1

        def state_rows(p, b):
            a = KK if b < 4 else AA
            return a[0:HD, p, 128 * (b % 4):128 * (b % 4) + 128]

        ctx.enter_context(nc.allow_non_contiguous_dma(reason="parameter vectors of a few hundred elements"))
        block = ctx.enter_context(nc.Block())
        n_out = [0]

        @block.sync
        def _(sp):
            def load(dst, src, s):
                sp.dma_start(dst, src).then_inc(s, 16)

            def store(dst, src, s=out_sem):
                sp.dma_start(dst, src).then_inc(s, 16)

            load(cT[:, 0, :], t['c_prompt'].rearrange("b (p c) -> p (b c)", c=DC), c_landed)
            load(cT[:, 1:NB + 1, :], t['c_sample'].rearrange("b (p c) -> p b c", c=DC), c_landed)

            def weights(n):
                kind, j = blocks[n]
                slot = wring[n % 3]
                if n >= 3:
                    s, v = block_used(n - 3)
                    sp.wait_ge(s, v)
                if kind == "ada":
                    src = t['w_ada'].rearrange("(p c) n -> p c n", c=DC)[:, :, 512 * j:512 * j + 512]
                elif kind == "in":
                    a, b = in_cols[j]
                    slot = slot[:, :, 0:b - a]
                    src = t['w_in'].rearrange("(p c) n -> p c n", c=DC)[:, :, a:b]
                elif kind == "gate":
                    src = t['w_in'].rearrange("(p c) n -> p c n", c=DC)[:, :, j:j + 512]
                elif kind == "out":
                    src = t['w_out'].rearrange("(c p) n -> p c n", p=128)[:, :, 512 * j:512 * j + 512]
                elif kind == "shared":
                    slot = slot.rearrange("p c n -> p (c n)")
                    load(slot[:, 0:2048].rearrange("p (c n) -> p c n", c=DC), t['w_sh_gate'].rearrange("(p c) n -> p c n", c=DC), w_landed[n % 3])
                    slot, src = slot[:, 2048:4096].rearrange("p (c n) -> p c n", c=DC), t['w_sh_up'].rearrange("(p c) n -> p c n", c=DC)
                elif kind == "down":
                    slot = slot.rearrange("p c n -> p (c n)")
                    load(slot[:, 2048:2560].rearrange("p (c n) -> p c n", c=DC), t['w_router'].rearrange("(p c) n -> p c n", c=DC), w_landed[n % 3])
                    slot, src = slot[:, 0:2048].rearrange("p (c n) -> p c n", c=2), t['w_sh_down'].rearrange("(p c) n -> p c n", c=2)
                load(slot, src, w_landed[n % 3])

            for n in range(3):
                weights(n)
            load(bada, t['b_ada'].rearrange("(a n) -> a n", a=1).broadcast_to([NB + 1, 6 * D]), b_landed)
            load(gains[:, 0, :], t['norm1_g'].rearrange("(a n) -> a n", a=1).broadcast_to([NB + 1, D]), g_landed)
            load(gains[:, 1, :], t['norm2_g'].rearrange("(a n) -> a n", a=1).broadcast_to([NB + 1, D]), g_landed)
            for i in range(NTP):
                load(x_all[:, i, :], t['x_prompt'][0, 128 * i:128 * i + 128, :], x_landed)
            load(x_all[0:NSM, NTP, :], t['x_sample'].rearrange("b t d -> (b t) d"), x_landed)
            load(sstate, t['state_shift'], x_landed)
            for n in range(3, 12):
                weights(n)
            sp.wait_ge(ada_out, 12)
            store(modD, mod[0:NB + 1, :], mod_stored)
            sp.wait_ge(mod_stored, 16)
            for k, j in enumerate((0, 1)):
                load(bcast[:, 0, k, :], modD[0:1, j * D:j * D + D].broadcast_to([128, D]), bc_landed)
                for b in range(NB):
                    load(bcast[8 * b:8 * b + 8, 1, k, :],
                         modD[b + 1:b + 2, j * D:j * D + D].broadcast_to([8, D]), bc_landed)
            for n in range(12, 15):
                weights(n)
            sp.wait_ge(h_ready, NTP)
            store(o['shift_prompt'], x_all[127:128, NTP - 1, :], shift_out)
            sp.wait_ge(h_ready, NTT)
            for b in range(NB):
                store(o['shift_sample'][b:b + 1, :], x_all[8 * b + 7:8 * b + 8, NTP, :], shift_out)
            for n in range(15, 18):
                weights(n)
            sp.wait_ge(ada_out, 12)
            load(lora_wa[0:64], t['w_w2'], lora_landed)
            load(lora_wa[64:128], t['w_a2'], lora_landed)
            load(lora_g, t['w_g2'], lora_landed)
            for n in range(18, 20):
                weights(n)
            for i in range(NTT):
                r = tile_rows(i)
                kd, vd, ld = [(o[n + '_prompt'].rearrange("a t h d -> (a t) (h d)")[128 * i:128 * i + 128] if n != 'logf'
                               else o['logf_prompt'].rearrange("a t h -> (a t) h")[128 * i:128 * i + 128]) if i < NTP else
                              (o[n + '_sample'].rearrange("a t h d -> (a t) (h d)") if n != 'logf'
                               else o['logf_sample'].rearrange("a t h -> (a t) h")) for n in ('k', 'v', 'logf')]
                sp.wait_ge(v_out, i + 1)
                store(vd, vtok[0:r, i, :], kv_stored)
                sp.wait_ge(kt_out, i + 1)
                store(kd, ktok[0:r, i, :], kv_stored)
                sp.wait_ge(lf_out, i + 1)
                store(ld, lftok[0:r, i, :], kv_stored)
            sp.wait_ge(s_ps, NTP)
            for p in range(NPAIR):
                for b in range(NB):
                    load(state_rows(p, b).rearrange("i (h j) -> i h j", h=2),
                         t['state_wkv'][b, 2 * p:2 * p + 2].rearrange("h i j -> i h j"), lora_landed)
            sp.wait_ge(w_out_, 1)
            store(o['wkv_prompt'][0].rearrange("h i j -> i h j"), prompt_state.rearrange("i (h j) -> i h j", h=H))
            for p in range(NPAIR):
                for half in range(2):
                    sp.wait_ge(w_out_, 2 + 2 * p + half)
                    for b in range(4 * half, 4 * half + 4):
                        store(o['wkv_sample'][b, 2 * p:2 * p + 2].rearrange("h i j -> i h j"),
                              state_rows(p, b).rearrange("i (h j) -> i h j", h=2))

            sp.wait_ge(lf_done, 3 + 1)
            for b in range(NB):
                store(revD[b].rearrange("h g s -> g h s"), rev[NPG * b:NPG * b + NPG], rev_stored)
            sp.wait_ge(rev_stored, 16 * NB)
            sp.wait_ge(out_sem, 16 * (1 + NPAIR * NB))
            load(revT, revD.rearrange("b h g s -> (b h) (g s)"), rev_landed)

            def pages(b, g, cache, dst, s):
                for k in range(4):
                    page = sp.value_load(t['page_table'][b:b + 1, 4 * g + k:4 * g + k + 1], min_val=0, max_val=159)
                    load(dst[:, k:k + 1, :], t[cache].rearrange("n s h d -> n s (h d)")[bass.ds(page, 1)].rearrange("n s c -> s n c"), s)

            def keys(b, g):
                q = 4 * b + g
                if q >= 2:
                    sp.wait_ge(kt_tr, 4 * (q - 2) + 4)
                pages(b, g, 'cache_k', kpage[q % 2], k_landed[q % 2])

            def values(b, g):
                q = 4 * b + g
                if q >= 2:
                    sp.wait_ge(vq_mm, q - 1)
                pages(b, g, 'cache_v', vpage[q % 2], v_landed[q % 2])

            for g in range(4):
                keys(0, g)
            for b in range(NB):
                for g in range(4):
                    if b + 1 < NB:
                        keys(b + 1, g)
                for g in range(4):
                    values(b, g)
            sp.wait_ge(kt_tr, 16 * NB)
            sp.wait_ge(ot_ps, NB)
            sp.wait_ge(at_oe, 16 + NB)
            for n in (20, 21):
                weights(n)
            load(w_brr, t['w_br_r'].rearrange("(c p) n -> p c n", p=128), br_landed)
            load(w_brf, t['w_br_f'].rearrange("(c p) n -> p c n", p=128), br_landed)
            weights(22)
            for i in range(NTP):
                load(x1[:, i, :], t['x_prompt'][0, 128 * i:128 * i + 128, :], x_landed)
            load(x1[0:NSM, NTP, :], t['x_sample'].rearrange("b t d -> (b t) d"), x_landed)
            weights(23)
            weights(24)
            sp.wait_ge(mg_out, DC)
            for k, j in enumerate((2, 3, 4)):
                load(bc2[:, k, 0, :], modD[0:1, j * D:j * D + D].broadcast_to([128, D]), bc_landed)
                for b in range(NB):
                    load(bc2[8 * b:8 * b + 8, k, 1, :],
                         modD[b + 1:b + 2, j * D:j * D + D].broadcast_to([8, D]), bc_landed)
            for n in range(25, 28):
                weights(n)
            for i in range(NTT):
                sp.wait_ge(h_ready, 5 + i + 1)
                store(h2D[128 * i:128 * i + tile_rows(i)], h2[0:tile_rows(i), i, :], mod_stored)

            load(ebias, t['e_bias'].rearrange("(a n) -> a n", a=1).broadcast_to([128, NE]), eb_landed)
            sp.wait_ge(pool_route, 1)
            store(slotD.rearrange("(p i) k -> p (i k)", p=128), fill, slot_filled)
            sp.wait_ge(tables, 1)
            store(itemD[0:1, 0:128].rearrange("a p -> p a"), item_i, items_stored)
            store(itemD[0:1, 128:129], n_i[0:1, :], items_stored)
            sp.wait_ge(slot_set, 16 * NTT * TOPK)
            load(slots, slotD.rearrange("(p i) k -> p (i k)", p=128), slots_landed)

            def expert(item, u):
                e = sp.value_load(itemD[0:1, bass.ds(item, 1)], min_val=0, max_val=NE - 1)
                return e

            def load_gate_up(e, u):
                for k, name in enumerate(('w_exp_gate', 'w_exp_up')):
                    load(wgu[u][:, k:k + 1].rearrange("p a c n -> p a (c n)"),
                         t[name][bass.ds(e, 1)].rearrange("e (p c) n -> p e (c n)", c=DC), gu_landed[u])

            def load_down(e, u):
                load(wdn[u].rearrange("p c n -> p (c n)").unsqueeze(1), t['w_exp_down'][bass.ds(e, 1)].rearrange("e (p c) n -> p e (c n)", c=2), dn_landed[u])

            sp.wait_ge(sd_ps, NTT)
            rest = n_items(sp)
            for u in range(2):
                e = expert(u, u)
                load_gate_up(e, u)
                load_down(e, u)
            with sp.Fori(0, rest + 2, 2) as i:
                for u in range(2):
                    e = expert(i + (2 + u), u)
                    sp.wait_ge(sg_ps, 5 + i + (u + 1))
                    load_gate_up(e, u)
                    sp.wait_ge(sd_ps, 5 + i + (u + 1))
                    load_down(e, u)
            sp.wait_ge(sd_out, 5 + rest + 4)
            load(g2b[:, 0, :], modD[0:1, 5 * D:6 * D].broadcast_to([128, D]), x_landed)
            for b in range(NB):
                load(g2b[8 * b:8 * b + 8, 1, :], modD[b + 1:b + 2, 5 * D:6 * D].broadcast_to([8, D]), x_landed)
            load(nfb, t['normf_g'].rearrange("(a n) -> a n", a=1).broadcast_to([128, D]), x_landed)
            for u in range(2):
                sp.wait_ge(y_stored[u], (rest + 4) * 8)
            for i in range(NTT):
                r = tile_rows(i)
                if i >= 2:
                    sp.wait_ge(yr_done, 4 + i - 1)
                load(ykb[i % 2][0:r], ykD.rearrange("(t k) d -> t k d", k=TOPK)[128 * i:128 * i + r], yk_landed[i % 2])
                if i >= 1:
                    sp.wait_ge(h_ready, 10 + i)
                    store(o['y_prompt'][0, 128 * (i - 1):128 * i], x1[:, i - 1, :])
            sp.wait_ge(h_ready, 10 + NTT)
            store(o['y_sample'].rearrange("b t d -> (b t) d"), x1[0:NSM, NTP, :])
            sp.wait_ge(out_sem, 16 * 38)

        @block.gpsimd
        def _(pool):
            params = [(mu_c, 'mu_shift'), (w0c, 'w0'), (a0c, 'a0'), (kkc, 'k_k'), (kac, 'k_a'), (rkc, 'r_k'),
                      (lwc, 'lnx_w'), (lbc, 'lnx_b')]
            for dst, name in params:
                src = t[name] if name != 'r_k' else t[name].rearrange("h d -> (h d)")
                pool.dma_start(dst, src.rearrange("(c p) -> p c", p=128)).then_inc(par_landed, 16)
            pool.dma_start(bf_c[0:H, :], t['b_f'].rearrange("(p c) -> p c", c=1)).then_inc(par_landed, 16)

            pool.dma_start(page_ids, t['page_table'].rearrange("b (g o) -> (b g) o", o=1)).then_inc(pg_ids, 16)
            n = [0]

            def then(ins):
                n[0] += 1
                ins.then_inc(order_pool, 1)
                pool.wait_ge(order_pool, n[0])

            def select(dst, pattern, base, mult, op=ALU.is_ge, fill=0.0):
                then(pool.affine_select(out=dst, in_=dst, compare_op=op, fill=fill, base=base, pattern=pattern,
                                        channel_multiplier=mult))

            then(pool.memset(ones, 1.0))
            then(pool.memset(ident, 0.0))
            select(ident, [[-1, 128]], 0, 1, ALU.not_equal, 1.0)
            then(pool.memset(up_incl, 1.0))
            select(up_incl, [[1, 128]], 0, -1)
            then(pool.memset(up_strict, 1.0))
            select(up_strict, [[1, 128]], -1, -1)
            then(pool.memset(low_neg, 0.0))
            select(low_neg, [[-1, 128]], 0, 1, fill=-BIG)
            then(pool.memset(same.rearrange("p a b -> p (a b)"), 1.0))
            for m in range(7):
                b = 2 ** m
                v = same[:, m, :].rearrange("p (k j) -> p k j", j=b)
                select(v, [[-b, 128 // b], [0, b]], 0, 1)
                select(v, [[b, 128 // b], [0, b]], b - 1, -1)
            then(pool.memset(segment, 1.0))
            then(pool.memset(segment[:, 0:NP_].rearrange("p (i s) -> p i s", s=128)[:, :, 0:1], 0.0))
            then(pool.memset(segment[:, NP_:NT].rearrange("p (i s) -> p i s", s=NS)[:, :, 0:1], 0.0))
            then(pool.memset(mask_s.rearrange("p a b -> p (a b)"), 0.0))
            then(pool.memset(neg_new.rearrange("p a b -> p (a b)"), -BIG))
            pool.memset(ss, 1.0).then_inc(pool_const, 1)

            for i in range(NTT):
                T = tile_rows(i)
                for m in range(levels(i)):
                    for g in range(2):
                        if m == 0:
                            pool.wait_ge(at_out, 8 * i + 4 * g + 4)
                            if i > 0:
                                pool.wait_ge(p_ps, lv(i - 1, levels(i - 1) - 1, g))
                        elif m == 1:
                            pool.wait_ge(t_add, lv(i, 0, g))
                        else:
                            pool.wait_ge(p_ps, lv(i, m - 1, g))
                        pool.tensor_tensor(ML[g][0:T, :, 0:T], AT[0:T, 4 * g:4 * g + 4, 0:T],
                                           level[0:T, m, 0:T].unsqueeze(1).broadcast_to([T, 4, T]), ALU.mult).then_inc(ml_done, 1)

            pool.wait_ge(pg_ids, 16)
            pool.wait_ge(yr_done, NPAIR)
            pool.indirect_dma_start(lf_pages.rearrange("g s h -> g (s h)"), None, t['cache_logf'].rearrange("n s h -> n (s h)"),
                                    bass.IndirectOffsetOnAxis(page_ids, 0)).then_inc(lf_landed, 16)

            pool.wait_ge(h_ready, 5 + NTT)
            then(pool.iota(iota64, [[1, NE]], base=0, channel_multiplier=0, allow_small_or_imprecise_dtypes=True))
            then(pool.iota(iota_p, [[1, 1]], base=0, channel_multiplier=1, allow_small_or_imprecise_dtypes=True))
            then(pool.iota(payload.rearrange("p (i k a) -> p i k a", i=NTT, k=TOPK)[:, :, :, 0:1], [[128, NTT], [0, TOPK], [0, 1]], base=0,
                           channel_multiplier=1))
            then(pool.iota(payload.rearrange("p (i k a) -> p i k a", i=NTT, k=TOPK)[:, :, :, 1:2], [[128 * TOPK, NTT], [1, TOPK], [0, 1]], base=0,
                           channel_multiplier=TOPK))
            then(pool.memset(valid, 1.0))
            then(pool.memset(valid[64:128, NTP:NTP + 1], 0.0))
            then(pool.memset(score.rearrange("p a b -> p (a b)"), 0.5))
            pool.memset(fill, NOWHERE).then_inc(pool_route, 1)
            pool.wait_ge(slot_filled, 16)
            pool.wait_ge(slots_in, 1)
            for k in range(NTT * TOPK):
                pool.indirect_dma_start(slotD, bass.IndirectOffsetOnAxis(pos_i[:, k:k + 1], 0), payload[:, 2 * k:2 * k + 2], None,
                                        bounds_check=128 * MAXI - 1, oob_is_err=False).then_inc(slot_set, 16)
            rest = n_items(pool)
            pool.wait_ge(slots_landed, 16)
            pool.wait_ge(sg_ps, NTT)
            pool.wait_ge(lg_ps, NTT)
            then(pool.memset(hg[0], 0.0))
            then(pool.memset(hg[1], 0.0))

            def gather(item, u, first=False):
                if not first:
                    pool.wait_ge(tr1, 22 + item - 1)
                pool.tensor_copy(g_idx[u], slots[:, bass.ds(item * 2, 1)]).then_inc(idx_g, 1)
                pool.wait_ge(idx_g, item + 1)
                pool.indirect_dma_start(hg[u], None, h2D, bass.IndirectOffsetOnAxis(g_idx[u], 0),
                                        bounds_check=item + (NT - 1), oob_is_err=False).then_inc(hg_landed[u], 16)

            def scatter(item, u, stored):
                if stored is not None:
                    pool.wait_ge(y_stored[u], stored)
                pool.tensor_copy(s_idx[u], slots[:, bass.ds(item * 2 + 1, 1)]).then_inc(idx_s, 1)
                pool.wait_ge(idx_s, item + 1)
                pool.wait_ge(y_a, item + 1)
                pool.wait_ge(sd_out, 5 + item + 1)
                pool.indirect_dma_start(ykD, bass.IndirectOffsetOnAxis(s_idx[u], 0), ye[u], None,
                                        bounds_check=item + (NT * TOPK - 1), oob_is_err=False).then_inc(y_stored[u], 16)

            gather(0, 0, True)
            gather(1, 1, True)
            gather(2, 0)
            scatter(0, 0, None)
            gather(3, 1)
            scatter(1, 1, None)
            with pool.Fori(2, rest + 4, 2) as i:
                gather(i + 2, 0)
                scatter(i, 0, i * 8)
                gather(i + 3, 1)
                scatter(i + 1, 1, i * 8)

        @block.scalar
        def _(act):
            n = [0]

            def then(ins):
                n[0] += 1
                ins.then_inc(order_act, 1)
                act.wait_ge(order_act, n[0])

            signalled = {at_ex.name: 32}

            def done(ins, s):
                signalled[s.name] = signalled.get(s.name, 0) + 1
                ins.then_inc(s, 1)
                act.wait_ge(s, signalled[s.name])

            act.wait_ge(c_landed, 32)
            act.activation(cE, cT, ACT.Exp, scale=-1.0).then_inc(c_exp, 1)
            act.wait_ge(x_landed, 16 * 6)
            act.wait_ge(pool_const, 1)
            for i in range(NTT):
                r = tile_rows(i)
                done(act.activation(sqjunk[0:r], x_all[0:r, i, :], ACT.Square, accum_out=ss[0:r, i:i + 1]), sq1)
            act.wait_ge(ms1, 1)
            act.activation(rstd, rstd, ACT.Sqrt).then_inc(sqrt1, 1)
            for i in range(NTT + 1):
                T = tile_rows(i) if i < NTT else NB
                for half in range(2):
                    act.wait_ge(tr1, 2 * i + half + 1)
                    src = psum[:, 2 + 2 * (i % 2) + half, 0:4 * T].rearrange("p (c s) -> p c s", c=4)
                    dst = hT[:, 4 * half:4 * half + 4, :]
                    act.activation(dst[:, :, 128 * i:128 * i + T] if i < NTT else dst[:, :, NT:], src, ACT.Copy).then_inc(ev1, 1)
            act.wait_ge(shift_out, 16 * (NB + 1))
            act.wait_ge(dve_const, 1)
            for m in range(RCH + 2 * NPAIR):
                act.wait_ge(pj_ps, m + 1)
                a, b = psum[:, 2 * (m % 3), :], psum[:, 2 * (m % 3) + 1, 0:NCOL - NP_]
                if m < RCH:
                    if m >= 2:
                        act.wait_ge(mixed, m - 1)
                    r = raw[m % 2]
                    act.activation(r[:, 1:NP_ + 1], a, ACT.Copy)
                    rs = r[:, NP_ + 1:].rearrange("p (b s) -> p b s", b=NB)
                    act.activation(rs[:, :, 1:], b[:, 0:NSM].rearrange("p (b s) -> p b s", b=NB), ACT.Copy)
                    act.activation(rs[:, :, 0], b[:, NSM:], ACT.Copy).then_inc(pj_out, 1)
                else:
                    k = (m - RCH) % NPAIR
                    dst, scale = (qT, HD ** -0.5) if m < RCH + NPAIR else (kT, 1.0)
                    act.activation(dst[:, k, 0:NP_], a, ACT.Copy, scale=scale)
                    act.activation(dst[:, k, NP_:], b[:, 0:NSM], ACT.Copy, scale=scale).then_inc(pj_out, 1)
            act.wait_ge(v_ps, 5 + 1)
            act.wait_ge(par_landed, 16 * 9)
            act.activation(fT[0:H, 0:NP_], psum[0:H, 0, :], ACT.Identity, bias=bf_c[0:H, :])
            act.activation(fT[0:H, NP_:], psum[0:H, 1, 0:NSM], ACT.Identity, bias=bf_c[0:H, :]).then_inc(f_act, 1)
            act.wait_ge(f_act, 1)
            then(act.activation(fabs[0:H], fT[0:H], ACT.Abs))
            then(act.activation(fabs[0:H], fabs[0:H], ACT.Exp, scale=-1.0))
            act.activation(fabs[0:H], fabs[0:H], ACT.Ln, bias=1.0).then_inc(f_act, 1)

            act.wait_ge(mixed, RCH)
            done(act.activation(PM[0:64, 12, :], PM[0:64, 12, :], ACT.Tanh), lora_in)
            done(act.activation(PM[:, 13, :], PM[:, 13, :], ACT.Sigmoid), lora_in)
            for q in range(3 * NPAIR):
                act.wait_ge(lora_ps, q + 1)
                p, k = q // 3, q % 3
                for a, b, bank in ((0, NP_, 2 * (q % 3)), (NP_, NT, 2 * (q % 3) + 1)):
                    src = psum[:, bank, 0:b - a]
                    if k == 0:
                        ins = act.activation(LW[:, p, a:b], src, ACT.Sigmoid, bias=w0c[:, p:p + 1])
                    elif k == 1:
                        ins = act.activation(AA[:, p, a:b], src, ACT.Sigmoid, bias=a0c[:, p:p + 1])
                    else:
                        ins = act.activation(GG[:, p, a:b], src, ACT.Copy)
                ins.then_inc(lora_out, 1)
            for p in range(NPAIR):
                act.wait_ge(kk_raw, p + 1)
                act.activation(BV[:, p, :], KK[:, p, :], ACT.Square).then_inc(kk_sq, 1)
            for p in range(NPAIR):
                act.wait_ge(kk_n2, p + 1)
                act.activation(BV[:, p, 0:NP_], psum[:, 2 * (p % 2), :], ACT.Sqrt)
                act.activation(BV[:, p, NP_:], psum[:, 2 * (p % 2) + 1, 0:NSM], ACT.Sqrt).then_inc(kk_norm, 1)
            for p in range(NPAIR):
                act.wait_ge(t1_ready, p + 1)
                if p >= 2:
                    act.wait_ge(prep_done, p - 1)
                act.activation(LW[:, p, :], LW[:, p, :], ACT.Exp)
                act.activation(exp_neg[p % 2], CC[:, p, :], ACT.Exp, scale=-1.0).then_inc(e_neg, 1)
                act.wait_ge(e_neg, p + 1)
                act.activation(e_mid[:, p, :], c_mid[:, p, :], ACT.Exp)
                act.activation(CC[:, p, :], CC[:, p, :], ACT.Exp).then_inc(e_ready, 1)
            for i in range(NTT):
                T = tile_rows(i)
                for p in range(NPAIR):
                    act.wait_ge(tm_ps, 4 * i + p + 1)
                    act.activation(TM[0:T, p].rearrange("s a b -> s (a b)"), psum[0:T, p % 2, 0:384], ACT.Copy).then_inc(tm_out, 1)
                for m in range(1, levels(i)):
                    for g in range(2):
                        act.wait_ge(p_ps, lv(i, m, g))
                        if lvp(i, m, g) > 2:
                            act.wait_ge(dt_ps, lvp(i, m, g) - 2)
                        act.activation(TP[g][0:T, :, 0:T], psum[0:T, 4 + g, :].rearrange("s (h t) -> s h t", h=4)[:, :, 0:T],
                                       ACT.Copy).then_inc(p_out, 1)
                if i < NTP:
                    act.wait_ge(r_ps, i + 1)
                    act.activation(Rb[:, 0::2, :], psum[:, 2, 0:256].rearrange("s (a b) -> s a b", a=NPAIR), ACT.Copy)
                    act.activation(Rb[:, 1::2, :], psum[:, 6, 0:256].rearrange("s (a b) -> s a b", a=NPAIR), ACT.Copy).then_inc(r_out, 1)
                    act.wait_ge(u_ps, i + 1)
                    act.activation(Ub.rearrange("s a b -> s (a b)"), psum[:, 3, :], ACT.Copy).then_inc(u_out, 1)
            for p in range(NPAIR):
                act.wait_ge(st_ps, p + 1)
                act.activation(rho[:, p, 0:512], psum[:, p % 2, :], ACT.Copy).then_inc(st_out, 1)
            act.wait_ge(ro_ps, 1)
            act.activation(ro_sb[:, 0], psum[:, 2, 0:256], ACT.Copy).then_inc(ro_out, 1)
            act.activation(ro_sb[:, 1], psum[:, 3, 0:256], ACT.Copy).then_inc(ro_out, 1)
            act.wait_ge(ro_ps, 1 + 1)
            act.activation(Rb[0:NSM].rearrange("s a b -> s (a b)"), psum[0:NSM, 4, :], ACT.Copy).then_inc(ro_out, 1)
            act.wait_ge(u_ps, NTP + 1)
            act.activation(Ub[0:NSM].rearrange("s a b -> s (a b)"), psum[0:NSM, 3, :], ACT.Copy).then_inc(u_out, 1)
            for q in range(1 + 2 * NPAIR):
                act.wait_ge(w_ps, q + 1)
                dst = prompt_state if q == 0 else (KK if q % 2 else AA)[0:HD, (q - 1) // 2, 0:512]
                act.activation(dst, psum[0:HD, 6 + q % 2, :], ACT.Copy).then_inc(w_out_, 1)

            for p in range(NPAIR):
                act.wait_ge(ln_in, p + 1)
                act.activation(khat[:, p, :], YT[:, p, :], ACT.Square).then_inc(ln_sq, 1)
            for p in range(NPAIR):
                act.wait_ge(ln_var, p + 1)
                act.activation(khat[:, p, 0:NP_], psum[:, 4 + 2 * (p % 2), :], ACT.Sqrt, bias=epsx, scale=1.0 / HD)
                act.activation(khat[:, p, NP_:], psum[:, 5 + 2 * (p % 2), 0:NSM], ACT.Sqrt, bias=epsx, scale=1.0 / HD).then_inc(ln_sd, 1)
            act.wait_ge(yr_done, NPAIR)
            for j in range(NTP * H):
                kw = 128 * (j // H + 1)
                act.wait_ge(at_mx, j + 1)
                if j >= 2:
                    act.wait_ge(at_tp, j - 1)
                act.activation(Pb[j % 2][:, 0:kw], psum[:, j % 2, 0:kw], ACT.Exp, bias=nmx[:, j % 2:j % 2 + 1],
                               accum_out=row_sum[:, j % 2:j % 2 + 1]).then_inc(at_ex, 1)
                if j >= 1:
                    act.wait_ge(at_tp, j)
                    if j >= 3:
                        act.wait_ge(at_o, j - 2)
                    kw = 128 * ((j - 1) // H + 1)
                    act.activation(PTb[(j - 1) % 2][:, 0:kw], psum[:, 2 + (j - 1) % 2, 0:kw], ACT.Copy).then_inc(at_pt, 1)
            act.wait_ge(at_tp, NTP * H)
            act.activation(PTb[1], psum[:, 3, :], ACT.Copy).then_inc(at_pt, 1)

            def evacuate_keys(q):
                for j in range(4 * q, 4 * q + 4, 2):
                    act.wait_ge(kt_tr, j + 1)
                    if j >= 2:
                        act.wait_ge(kq_mm, j - 1)
                    act.activation(KTb[0], psum[:, 0, :], ACT.Copy).then_inc(kte[0], 1)

            act.wait_ge(x_ps, H)
            for b in range(NB + 1):
                if b < NB:
                    for g in range(4):
                        evacuate_keys(4 * b + g)
                if b >= 2:
                    act.wait_ge(ot_ps, b - 1)
                    for e in range(2):
                        sl, c0 = slice(64 * e, 64 * e + 64), NP_ + NS * (b - 2)
                        ins = act.activation(yfT[sl, :, c0:c0 + NS],
                                             psum[sl, 7, NS * e:NS * e + 320].rearrange("a (p x) -> a p x", x=80)[:, :, 0:NS], ACT.Copy)
                    ins.then_inc(yf_out, 1)
                if b >= 1:
                    for m in range(3):
                        r, w = (128, 512) if m < 2 else (64, 64)
                        act.wait_ge(at_tp, 32 + 3 * (b - 1) + m + 1)
                        if b >= 3:
                            act.wait_ge(at_o, 32 + b - 2)
                        act.activation(PTs[(b - 1) % 2].rearrange("s a b -> s (a b)")[0:r, 512 * m:512 * m + w],
                                       psum[0:r, 5 + (3 * (b - 1) + m) % 2, 0:w], ACT.Copy).then_inc(at_pt, 1)
                if b < NB:
                    act.wait_ge(at_mx, 32 + b + 1)
                    done(act.activation(Ssb[b % 2], Ssb[b % 2], ACT.Exp, bias=nmx[0:64, b % 2:b % 2 + 1], accum_out=row_sum[0:64, b % 2:b % 2 + 1]), at_ex)
            act.wait_ge(ot_ps, NB)
            for e in range(2):
                sl, c0 = slice(64 * e, 64 * e + 64), NP_ + NS * (NB - 1)
                ins = act.activation(yfT[sl, :, c0:c0 + NS],
                                     psum[sl, 7, NS * e:NS * e + 320].rearrange("a (p x) -> a p x", x=80)[:, :, 0:NS], ACT.Copy)
            ins.then_inc(yf_out, 1)
            for m in range(DC):
                for k in range(2):
                    j = 4 * m + 2 * k
                    act.wait_ge(mg_ps, j + 1)
                    if m >= 1:
                        act.wait_ge(mg_out, m)
                    b0 = 2 * (j % 4)
                    act.activation(sg[k][:, 0:NP_], psum[:, b0, :], ACT.Sigmoid)
                    act.activation(sg[k][:, NP_:], psum[:, b0 + 1, 0:NSM], ACT.Sigmoid).then_inc(mg_sg, 1)
            act.wait_ge(x1_done, 2 * NTT)
            for i in range(NTT):
                r = tile_rows(i)
                done(act.activation(junk2[0:r], x1[0:r, i, :], ACT.Square, accum_out=ss[0:r, i:i + 1]), sq1)
            act.wait_ge(ms1, 1 + 1)
            act.activation(rstd, rstd, ACT.Sqrt).then_inc(sqrt1, 1)
            for i in range(NTT):
                T = tile_rows(i)
                for half in range(2):
                    act.wait_ge(tr1, 12 + 2 * i + half + 1)
                    src = psum[:, 2 * (i % 2) + half, 0:4 * T].rearrange("p (c s) -> p c s", c=4)
                    act.activation(hT[:, 4 * half:4 * half + 4, 128 * i:128 * i + T], src, ACT.Copy).then_inc(ev1, 1)
            act.wait_ge(pool_route, 1)
            for i in range(NTT):
                T = tile_rows(i)
                act.wait_ge(lg_ps, i + 1)
                act.activation(score[0:T, i, :], psum[0:T, 6 + i % 2, 0:NE], ACT.Sigmoid).then_inc(f_act, 1)
            for i in range(NTT):
                T = tile_rows(i)
                act.wait_ge(sg_ps, i + 1)
                if i >= 2:
                    act.wait_ge(sg_mul, i - 1)
                act.activation(sil_s[i % 2][0:T], psum[0:T, 4 + i % 2, 0:EFF], ACT.Silu).then_inc(sg_act, 1)
                act.wait_ge(sg_tr, i + 1)
                if i >= 2:
                    act.wait_ge(sd_ps, i - 1)
                act.activation(actT_s[i % 2][:, :, 0:T], psum[:, 6, 0:2 * T].rearrange("p (c s) -> p c s", c=2), ACT.Copy).then_inc(sg_at, 1)

            def turned_rows(item, u, first=False):
                act.wait_ge(tr1, 22 + item + 1)
                if not first:
                    act.wait_ge(sg_ps, 5 + item - 1)
                act.activation(hgT[u][:, 0:4, :].rearrange("p c s -> p (c s)"), psum[:, 0, :], ACT.Copy).then_inc(ev1, 1)

            def silu(item, u, first=False):
                act.wait_ge(sg_ps, 5 + item + 1)
                if not first:
                    act.wait_ge(sg_mul, 5 + item - 1)
                act.activation(sile[u], psum[:, 2 + u, 0:EFF], ACT.Silu).then_inc(sg_act, 1)

            def turned_act(item, u, first=False):
                act.wait_ge(sg_tr, 5 + item + 1)
                if not first:
                    act.wait_ge(sd_ps, 5 + item - 1)
                act.activation(acteT[u].rearrange("p c s -> p (c s)"), psum[:, 4, 0:256], ACT.Copy).then_inc(sg_at, 1)

            def expert_out(item, u, stored=None):
                act.wait_ge(sd_ps, 5 + item + 1)
                if stored is not None:
                    act.wait_ge(y_stored[u], stored)
                act.activation(ye[u][:, 0:512], psum[:, 5, :], ACT.Copy).then_inc(y_a, 1)

            rest = n_items(act)
            act.wait_ge(f_act, 2 + NTT)
            turned_rows(0, 0, True)
            silu(0, 0, True)
            turned_rows(1, 1, True)
            silu(1, 1, True)
            turned_act(0, 0, True)
            turned_rows(2, 0)
            expert_out(0, 0)
            silu(2, 0)
            turned_act(1, 1, True)
            turned_rows(3, 1)
            expert_out(1, 1)
            silu(3, 1)
            turned_act(2, 0)
            turned_rows(4, 0)
            expert_out(2, 0, 16)
            with act.Fori(4, rest + 4, 2) as i:
                silu(i, 0)
                turned_act(i - 1, 1)
                turned_rows(i + 1, 1)
                expert_out(i - 1, 1, (i - 2) * 8)
                silu(i + 1, 1)
                turned_act(i, 0)
                turned_rows(i + 2, 0)
                expert_out(i, 0, i * 8)
            turned_act(rest + 3, 1)
            expert_out(rest + 3, 1, (rest + 2) * 8)
            for i in range(NTT):
                r = tile_rows(i)
                act.wait_ge(x1_done, 10 + i + 1)
                done(act.activation(junk2[0:r], x1[0:r, i, :], ACT.Square, accum_out=ss[0:r, i:i + 1]), sq1)
                act.wait_ge(ms1, 2 + i + 1)
                act.activation(rstd[0:r, i:i + 1], rstd[0:r, i:i + 1], ACT.Sqrt).then_inc(sqrt1, 1)

        @block.vector
        def _(dve):
            n = [0]

            def then(ins):
                n[0] += 1
                ins.then_inc(order_dve, 1)
                dve.wait_ge(order_dve, n[0])

            signalled = {h_ready.name: NTT, at_oe.name: 16, lf_done.name: 1}

            def done(ins, s):
                signalled[s.name] = signalled.get(s.name, 0) + 1
                ins.then_inc(s, 1)
                dve.wait_ge(s, signalled[s.name])

            dve.wait_ge(c_exp, 1)
            then(dve.tensor_scalar(cE, cE, 1.0, None, ALU.add))
            then(dve.reciprocal(cE, cE))
            dve.tensor_tensor(cT, cT, cE, ALU.mult).then_inc(c_ready, 1)
            dve.wait_ge(pool_const, 1)
            for m in range(7):
                then(dve.tensor_tensor(level[:, m, :], same[:, m + 1, :], same[:, m, :], ALU.subtract))
                then(dve.tensor_tensor(level[:, m, :], level[:, m, :], up_strict, ALU.mult))
            for k, m in enumerate((up_strict, up_incl, up_strict, up_incl)):
                dve.tensor_copy(mask_p[:, k, :], m)
                then(dve.tensor_tensor(mask_s[:, k, :], m, same[:, 3, :], ALU.mult))
            then(dve.tensor_copy(blk64, same[:, 6, :]))
            then(dve.tensor_copy(head_rows[0:64], ident[0:64, 0:64].rearrange("p (b h) -> p b h", b=NB).unsqueeze(3)
                                 .broadcast_to([64, NB, H, NS])))
            then(dve.memset(cum, 0.0))
            then(dve.memset(head8.rearrange("p a b -> p (a b)"), 0.0))
            then(dve.tensor_copy(head8[0:H], ident[0:H, 0:H].unsqueeze(2).broadcast_to([H, H, NS])))
            then(dve.tensor_scalar(lf_tmp[0:64], low_neg[0:64, 0:64], 1.0 / BIG, 1.0, ALU.mult, ALU.add))
            then(dve.tensor_tensor(lf_tmp[0:64], lf_tmp[0:64], same[0:64, 3, 0:64], ALU.mult))
            then(dve.tensor_reduce(tri8[0:64], lf_tmp[0:64].rearrange("p (k j) -> p j k", j=NS), AX.X, ALU.add))
            for b in range(NB):
                dve.tensor_scalar(neg_new[0:64, b, NS * b:NS * b + NS], tri8[0:64], -1.0, BIG, ALU.add, ALU.mult)
            then(dve.memset(eps1, EPS))
            then(dve.tensor_scalar(lower16, up_incl, -1.0, 1.0, ALU.mult, ALU.add))
            then(dve.tensor_tensor(lower16, lower16, same[:, 4, :], ALU.mult))
            then(dve.memset(epsx, LNX_EPS))
            dve.wait_ge(par_landed, 16 * 9)
            then(dve.tensor_scalar(ka1, kac, -1.0, 1.0, ALU.mult, ALU.add))
            dve.wait_ge(b_landed, 16)
            dve.wait_ge(g_landed, 32)
            for j in range(12):
                dve.wait_ge(ada_ps, j + 1)
                dst = mod[0:NB + 1, 512 * j:512 * j + 512]
                ins = dve.tensor_tensor(dst, psum[0:NB + 1, j % 2, :], bada[:, 512 * j:512 * j + 512], ALU.add)
                if j // 2 in (1, 4):
                    then(ins)
                    ins = dve.scalar_tensor_tensor(dst, dst, 1.0, gains[:, j // 8, 512 * (j % 2):512 * (j % 2) + 512],
                                                   ALU.add, ALU.mult)
                ins.then_inc(ada_out, 1)
            dve.wait_ge(sq1, NTT)
            dve.tensor_scalar(rstd, ss, 1.0 / D, EPS, ALU.mult, ALU.add).then_inc(ms1, 1)
            dve.wait_ge(sqrt1, 1)
            then(dve.reciprocal(rstd, rstd))
            dve.wait_ge(bc_landed, 16 * 2 * (NB + 1))
            for i in range(NTT):
                r, kind = tile_rows(i), i // NTP
                x = x_all[0:r, i, :]
                then(dve.scalar_tensor_tensor(x, x, rstd[0:r, i:i + 1], bcast[0:r, kind, 1, :], ALU.mult, ALU.mult))
                dve.tensor_tensor(x, x, bcast[0:r, kind, 0, :], ALU.add).then_inc(h_ready, 1)
            for k in range(2):
                ins = dve.memset(raw[k][:, 0:1], 0.0)
            ins.then_inc(dve_const, 1)
            dve.wait_ge(mod_stored, 16)
            for m in range(RCH):
                dve.wait_ge(pj_out, m + 1)
                r, mu = raw[m % 2], mu_c[:, m:m + 1]
                dst, dst_s = PM[:, m, 0:NP_], PM[:, m, NP_:].rearrange("p (b s) -> p b s", b=NB)
                rs = r[:, NP_ + 1:].rearrange("p (b s) -> p b s", b=NB)
                dve.tensor_tensor(dst, r[:, 0:NP_], r[:, 1:NP_ + 1], ALU.subtract)
                then(dve.tensor_tensor(dst_s, rs[:, :, 0:NS], rs[:, :, 1:], ALU.subtract))
                dve.scalar_tensor_tensor(dst, dst, mu, r[:, 1:NP_ + 1], ALU.mult, ALU.add)
                dve.scalar_tensor_tensor(dst_s, dst_s, mu, rs[:, :, 1:], ALU.mult, ALU.add).then_inc(mixed, 1)
            for i in range(NTT):
                dve.wait_ge(v_ps, i + 1)
                r = tile_rows(i)
                dve.tensor_copy(vtok[0:r, i, :], psum[0:r, 6 + i % 2, :]).then_inc(v_out, 1)
            dve.wait_ge(f_act, 2)
            dve.scalar_tensor_tensor(fT[0:H], fT[0:H], 0.0, fabs[0:H], ALU.min, ALU.subtract).then_inc(lf_done, 1)
            dve.wait_ge(lf_done, 1)
            dve.tensor_tensor_scan(cum[0:H, 0:NP_], ones[0:H, 0:1].broadcast_to([H, NP_]), fT[0:H, 0:NP_], 0.0, ALU.mult, ALU.add)
            then(dve.tensor_tensor_scan(cum[0:H, NP_:], segment[0:H, NP_:], fT[0:H, NP_:], 0.0, ALU.mult, ALU.add))
            done(dve.tensor_scalar(cum[0:H], cum[0:H], -1.0, None, ALU.mult), lf_done)
            for i in range(NTT):
                r = tile_rows(i)
                dve.wait_ge(kt_ps, i + 1)
                dve.tensor_copy(ktok[0:r, i, :], psum[0:r, 2 + i % 2, :]).then_inc(kt_out, 1)
                dve.wait_ge(lf_ps, i + 1)
                dve.tensor_copy(lftok[0:r, i, :], psum[0:r, 4 + i % 2, 0:H]).then_inc(lf_out, 1)

            for p in range(NPAIR):
                dve.wait_ge(lora_out, 3 * p + 1)
                then(dve.tensor_scalar(LW[:, p, :], LW[:, p, :], -DECAY_MAX, None, ALU.mult))
                then(dve.tensor_tensor_scan(CC[:, p, :], segment, LW[:, p, :], 0.0, ALU.mult, ALU.add))
                then(dve.tensor_copy(c_mid[:, p, :], CC[:, p, 63:NP_:128]))
                c3 = CC[:, p, 0:NP_].rearrange("p (i s) -> p i s", s=128)
                then(dve.tensor_tensor(c3, c3, c_mid[:, p, :].unsqueeze(2).broadcast_to([128, NTP, 128]), ALU.subtract))
                done(dve.tensor_scalar(KK[:, p, :], PM[:, NPAIR + p, :], kkc[:, p:p + 1], None, ALU.mult), kk_raw)
            for p in range(NPAIR):
                r, k = PM[:, p, :], PM[:, NPAIR + p, :]
                dve.wait_ge(kk_norm, p + 1)
                then(dve.tensor_scalar(BV[:, p, :], BV[:, p, :], 1e-12, None, ALU.max))
                then(dve.reciprocal(BV[:, p, :], BV[:, p, :]))
                then(dve.tensor_tensor(KK[:, p, :], KK[:, p, :], BV[:, p, :], ALU.mult))
                dve.wait_ge(lora_out, 3 * p + 2)
                then(dve.tensor_scalar(BV[:, p, :], AA[:, p, :], kac[:, p:p + 1], ka1[:, p:p + 1], ALU.mult, ALU.add))
                then(dve.tensor_tensor(k, k, BV[:, p, :], ALU.mult))
                done(dve.scalar_tensor_tensor(BV[:, p, :], r, rkc[:, p:p + 1], k, ALU.mult, ALU.mult), rk_in)
                done(dve.tensor_tensor(LW[:, p, :], CC[:, p, :], LW[:, p, :], ALU.subtract), t1_ready)
            for p in range(NPAIR):
                r, k = PM[:, p, :], PM[:, NPAIR + p, :]
                then(dve.tensor_tensor(AA[:, p, :], AA[:, p, :], KK[:, p, :], ALU.mult))
                dve.wait_ge(e_ready, p + 1)
                dve.tensor_tensor(KK[:, p, :], KK[:, p, :], LW[:, p, :], ALU.mult)
                dve.scalar_tensor_tensor(AA[:, p, :], AA[:, p, :], -1.0, exp_neg[p % 2], ALU.mult, ALU.mult)
                dve.tensor_tensor(k, k, exp_neg[p % 2], ALU.mult)
                dve.tensor_tensor(r, r, CC[:, p, :], ALU.mult)
                dve.wait_ge(rk_ps, p + 1)
                dve.tensor_tensor(BV[:, p, 0:NP_], psum[:, 4 + 2 * (p % 2), :], PM[:, 2 * NPAIR + p, 0:NP_], ALU.mult)
                done(dve.tensor_tensor(BV[:, p, NP_:], psum[:, 5 + 2 * (p % 2), 0:NSM], PM[:, 2 * NPAIR + p, NP_:],
                                       ALU.mult), prep_done)
            dve.wait_ge(kv_stored, 16 * 3 * NTT)
            for i in range(NTT):
                T = tile_rows(i)
                mask = mask_p if i < NTP else mask_s
                for h in range(H):
                    dve.wait_ge(at_ps, 8 * i + h + 1)
                    dve.tensor_tensor(AT[0:T, h].rearrange("s (a t) -> s a t", a=4)[:, :, 0:T],
                                      psum[0:T, 2 + h % 2, :].rearrange("s (a t) -> s a t", a=4)[:, :, 0:T],
                                      mask[0:T, :, 0:T], ALU.mult).then_inc(at_out, 1)
                for m in range(levels(i)):
                    for g in range(2):
                        if m == 0:
                            dve.wait_ge(p_ps, lv(i, 0, g))
                            idb = ident[0:T, 0:T].unsqueeze(1).broadcast_to([T, 4, T])
                            dve.tensor_tensor(TIg[g][0:T, :, 0, 0:T],
                                              psum[0:T, 4 + g, :].rearrange("s (h t) -> s h t", h=4)[:, :, 0:T], idb, ALU.add)
                            done(dve.tensor_tensor(TIg[g][0:T, :, 1, 0:T], ML[g][0:T, :, 0:T], idb, ALU.add), t_add)
                            continue
                        dve.wait_ge(dt_ps, lvp(i, m, g))
                        if m < levels(i) - 1:
                            for k in range(2):
                                dst = TIg[g][0:T, 2 * k:2 * k + 2, :, 0:T]
                                src = psum[0:T, (6, 0)[g] + k, :].rearrange("s (h a t) -> s h a t", h=2, a=2)[:, :, :, 0:T]
                                ins = dve.tensor_tensor(dst, dst, src, ALU.add)
                        else:
                            dst = TIg[g][0:T, :, 1, 0:T]
                            ins = dve.tensor_tensor(dst, dst, psum[0:T, (6, 0)[g], :].rearrange("s (h t) -> s h t", h=4)[:, :, 0:T],
                                                    ALU.add)
                        done(ins, t_add)
                if i < NTP:
                    if i == 0:
                        done(dve.memset(S0.rearrange("p a b -> p (a b)"), 0.0), s0_ready)
                    else:
                        done(dve.tensor_tensor(S0, Sst, e_mid[:, :, i:i + 1].broadcast_to([128, NPAIR, HD]), ALU.mult), s0_ready)
                    dve.wait_ge(y_ps, i + 1)
                    dve.tensor_copy(YT[:, :, 128 * i:128 * i + 128], psum[:, 4, :].rearrange("p (a t) -> p a t", a=NPAIR)).then_inc(y_out, 1)
                    dve.wait_ge(s_ps, i + 1)
                    then(dve.tensor_tensor(Sst, S0, psum[:, 5, 0:256].rearrange("p (a t) -> p a t", a=NPAIR), ALU.add))
                    done(dve.tensor_tensor(Sst, Sst, CC[:, :, 128 * i + 127:128 * i + 128].broadcast_to([128, NPAIR, HD]), ALU.mult), s_out)
            dve.wait_ge(ro_ps, 2 + 1)
            dve.wait_ge(ro_out, 2 + 1)
            done(dve.tensor_tensor(Rb[0:NSM], Rb[0:NSM], psum[0:NSM, 5, :].rearrange("s (h i) -> s h i", h=H), ALU.add), r_out_s)
            dve.wait_ge(y_ps, NTP + 1)
            dve.wait_ge(ro_out, 2)
            done(dve.tensor_tensor(YT[:, :, NP_:], psum[:, 6, 0:256].rearrange("p (a t) -> p a t", a=NPAIR),
                              ro_sb[:, 1].rearrange("p (a t) -> p a t", a=NPAIR), ALU.add), y_out)
            own = same[0:NSM, 3, 0:NSM:NS].unsqueeze(2).broadcast_to([NSM, NB, HD])
            dve.wait_ge(u_out, NTP + 1)
            for h in range(H):
                if h >= 2:
                    dve.wait_ge(x_ps, h - 1)
                xv, xu = khat[0:NSM, 2 * (h % 2), 0:512], khat[0:NSM, 2 * (h % 2) + 1, 0:512]
                dve.tensor_tensor(xv.rearrange("s (b i) -> s b i", b=NB),
                                  TM[0:NSM, h // 2, 0, 64 * (h % 2):64 * (h % 2) + 64].unsqueeze(1).broadcast_to([NSM, NB, HD]), own, ALU.mult)
                done(dve.tensor_tensor(xu.rearrange("s (b i) -> s b i", b=NB),
                                       Ub[0:NSM, h].unsqueeze(1).broadcast_to([NSM, NB, HD]), own, ALU.mult), x_ready)
                if h % 2 == 1:
                    p = h // 2
                    dve.wait_ge(x_ps, h + 1)
                    st = rho[:, p, 0:512]
                    then(dve.tensor_tensor(st, st, psum[:, p % 2, :], ALU.add))
                    st3 = st.rearrange("p (b i) -> p b i", b=NB)
                    done(dve.tensor_tensor(st3, st3, CC[:, p, NP_ + NS - 1:NT:NS].unsqueeze(2).broadcast_to([128, NB, HD]), ALU.mult), x_out)

            for p in range(NPAIR):
                dve.wait_ge(ln_mu, p + 1)
                dve.scalar_tensor_tensor(YT[:, p, 0:NP_], psum[:, 2 * (p % 2), :], -1.0 / HD, YT[:, p, 0:NP_], ALU.mult, ALU.add)
                done(dve.scalar_tensor_tensor(YT[:, p, NP_:], psum[:, 2 * (p % 2) + 1, 0:NSM], -1.0 / HD, YT[:, p, NP_:], ALU.mult, ALU.add), ln_in)
            for p in range(NPAIR):
                y = YT[:, p, :]
                dve.wait_ge(ln_sd, p + 1)
                then(dve.reciprocal(khat[:, p, :], khat[:, p, :]))
                then(dve.tensor_tensor(y, y, khat[:, p, :], ALU.mult))
                then(dve.tensor_scalar(y, y, lwc[:, p:p + 1], lbc[:, p:p + 1], ALU.mult, ALU.add))
                then(dve.tensor_tensor(y, y, BV[:, p, :], ALU.add))
                done(dve.tensor_tensor(y, y, GG[:, p, :], ALU.mult), yr_done)

            def past_sums():
                dve.wait_ge(lf_landed, 16)
                for h in range(H):
                    ins = dve.tensor_tensor_scan(rev[:, h, :], ones, lf_pages[:, :, h], 0.0, ALU.mult, ALU.add)
                then(ins)
                done(dve.tensor_copy(sum_off[:, 0:H], rev[:, :, PG - 1]), lf_done)
                dve.wait_ge(rev_ps, 1)
                then(dve.tensor_tensor(sum_off[:, H:], sum_off[:, 0:H], psum[:, 7, 0:H], ALU.add))
                for h in range(H):
                    ins = dve.tensor_scalar(rev[:, h, :], rev[:, h, :], -1.0, sum_off[:, H + h:H + h + 1], ALU.mult, ALU.add)
                done(ins, lf_done)
                dve.wait_ge(out_sem, 16 * (1 + NPAIR * NB))
                then(dve.memset(qblk, 0.0))
                for b in range(NB):
                    for p in range(NPAIR):
                        for e in range(2):
                            sl, c0 = slice(64 * e, 64 * e + 64), 256 * b + 80 * p + 8 * e
                            ins = dve.tensor_copy(qblk[sl, c0:c0 + NS], qT[sl, p, NP_ + NS * b:NP_ + NS * b + NS])
                done(ins, lf_done)

            def evacuate_pair(j):
                dve.wait_ge(at_o, j + 1)
                p, qt = (j % H) // 2, j // H
                dve.tensor_copy(yfT[:, p, 128 * qt:128 * qt + 128], psum[:, 4 + (j // 2) % 2, 0:128]).then_inc(at_oe, 1)

            for j in range(NTP * H):
                kw = 128 * (j // H + 1)
                dve.wait_ge(at_sc, j + 1)
                if j >= 2:
                    dve.wait_ge(at_ex, j - 1)
                done(dve.tensor_reduce(nmx[:, j % 2:j % 2 + 1], psum[:, j % 2, 0:kw], AX.X, ALU.max, negate=True), at_mx)
                dve.wait_ge(at_ex, j + 1)
                then(dve.reciprocal(row_sum[:, j % 2:j % 2 + 1], row_sum[:, j % 2:j % 2 + 1]))
                done(dve.tensor_scalar(Pb[j % 2][:, 0:kw], Pb[j % 2][:, 0:kw], row_sum[:, j % 2:j % 2 + 1], None, ALU.mult), at_pn)
                if j >= 2 and j % 2 == 0:
                    evacuate_pair(j - 1)
            evacuate_pair(NTP * H - 1)
            past_sums()

            def sample_tail(b):
                dve.wait_ge(at_o, 32 + b + 1)
                if b >= 1:
                    dve.wait_ge(ot_ps, b)
                done(dve.tensor_scalar(Osb, psum[0:64, 7, :], row_inv[0:64, b % 2:b % 2 + 1], None, ALU.mult), at_oe)

            for b in range(NB):
                for g in range(4):
                    q = 4 * b + g
                    for j in range(4 * q + 1, 4 * q + 4, 2):
                        dve.wait_ge(kt_tr, j + 1)
                        if j >= 3:
                            dve.wait_ge(kq_mm, j - 1)
                        dve.tensor_copy(KTb[1], psum[:, 1, :]).then_inc(kte[1], 1)
                    dve.wait_ge(kq_mm, 4 * q + 4)
                    if b >= 2:
                        dve.wait_ge(at_tp, 32 + 3 * (b - 1))
                    dve.tensor_copy(Ssb[b % 2][:, 512 * g:512 * g + 512], psum[0:64, 2 + q % 2, :]).then_inc(sc_out, 1)
                dve.wait_ge(nw_ps, b + 1)
                done(dve.tensor_copy(Ssb[b % 2][:, PAST:], psum[0:64, 4, 0:64]), nw_out)
                if b >= 2:
                    dve.wait_ge(at_ex, 32 + b - 1)
                done(dve.tensor_reduce(nmx[0:64, b % 2:b % 2 + 1], Ssb[b % 2], AX.X, ALU.max, negate=True), at_mx)
                if b >= 1:
                    sample_tail(b - 1)
                dve.wait_ge(at_ex, 32 + b + 1)
                then(dve.reciprocal(row_inv[0:64, b % 2:b % 2 + 1], row_sum[0:64, b % 2:b % 2 + 1]))
            sample_tail(NB - 1)
            for m in range(DC):
                for k in range(2):
                    j = 4 * m + 2 * k + 1
                    dve.wait_ge(mg_ps, j + 1)
                    dve.wait_ge(mg_sg, 2 * m + k + 1)
                    b0 = 2 * (j % 4)
                    dst = (mergedT[:, m, :], mt2)[k]
                    dve.tensor_tensor(dst[:, 0:NP_], psum[:, b0, :], sg[k][:, 0:NP_], ALU.mult)
                    then(dve.tensor_tensor(dst[:, NP_:], psum[:, b0 + 1, 0:NSM], sg[k][:, NP_:], ALU.mult))
                done(dve.tensor_tensor(mergedT[:, m, :], mergedT[:, m, :], mt2, ALU.add), mg_out)
            dve.wait_ge(x_landed, 96 + 16 * NTT)
            dve.wait_ge(bc_landed, 288 + 16 * 3 * (NB + 1))
            for half in range(2):
                for i in range(NTT):
                    r, kind, q = tile_rows(i), i // NTP, NTT * half + i
                    dve.wait_ge(xo_ps, q + 1)
                    c = slice(512 * half, 512 * half + 512)
                    then(dve.tensor_tensor(xo_tmp[0:r], psum[0:r, q % 4, :], bc2[0:r, 0, kind, c], ALU.mult))
                    done(dve.tensor_tensor(x1[0:r, i, c], x1[0:r, i, c], xo_tmp[0:r], ALU.add), x1_done)
            dve.wait_ge(sq1, 5 + NTT)
            dve.tensor_scalar(rstd, ss, 1.0 / D, EPS, ALU.mult, ALU.add).then_inc(ms1, 1)
            dve.wait_ge(sqrt1, 1 + 1)
            then(dve.reciprocal(rstd, rstd))
            for i in range(NTT):
                r, kind = tile_rows(i), i // NTP
                then(dve.scalar_tensor_tensor(h2[0:r, i, :], x1[0:r, i, :], rstd[0:r, i:i + 1], bc2[0:r, 2, kind, :], ALU.mult, ALU.mult))
                done(dve.tensor_tensor(h2[0:r, i, :], h2[0:r, i, :], bc2[0:r, 1, kind, :], ALU.add), h_ready)
            for i in range(NTT):
                T = tile_rows(i)
                dve.wait_ge(sg_act, i + 1)
                if i >= 2:
                    dve.wait_ge(sg_tr, i - 1)
                dve.tensor_tensor(act_s[i % 2][0:T], sil_s[i % 2][0:T], psum[0:T, 4 + i % 2, EFF:2 * EFF], ALU.mult).then_inc(sg_mul, 1)
                dve.wait_ge(sd_ps, i + 1)
                if i == 0:
                    dve.wait_ge(mod_stored, 16 + 16 * NTT)
                    dve.wait_ge(tr1, 12 + 2 * NTT)
                dve.tensor_copy(h2[0:T, i, 0:512], psum[0:T, 0 + 2 * (i % 2), :])
                dve.tensor_copy(h2[0:T, i, 512:], psum[0:T, 1 + 2 * (i % 2), :]).then_inc(sd_out, 1)

            dve.wait_ge(f_act, 2 + NTT)
            dve.wait_ge(eb_landed, 16)
            eb = ebias.unsqueeze(1).broadcast_to([128, NTT, NE])
            then(dve.tensor_tensor(biased, score, eb, ALU.add))
            for i in range(NTT):
                for g in range(8):
                    ins = dve.max(top8[:, i, g, :], biased[:, i, 8 * g:8 * g + 8])
            then(ins)
            then(dve.tensor_tensor(gscore, top8[:, :, :, 0], top8[:, :, :, 1], ALU.add))
            for i in range(NTT):
                then(dve.max(gtop[:, i, :], gscore[:, i, :]))
                then(dve.max_index(gidx_u[:, i, :], gtop[:, i, :], gscore[:, i, :]))
            then(dve.tensor_copy(gidx, gidx_u))
            then(dve.tensor_tensor(geq, iota64[:, 0:8].unsqueeze(1).unsqueeze(3).broadcast_to([128, NTT, 8, 4]),
                                   gidx[:, :, 0:4].unsqueeze(2).broadcast_to([128, NTT, 8, 4]), ALU.is_equal))
            then(dve.tensor_reduce(gmask, geq, AX.X, ALU.add))
            then(dve.tensor_scalar(gpen, gmask, -1.0, BIG, ALU.add, ALU.mult))
            gm = [a.rearrange("p i g -> p (i g)").unsqueeze(2).broadcast_to([128, NTT * 8, 8]) for a in (gmask, gpen)]
            m3 = masked.rearrange("p i (g j) -> p (i g) j", g=8)
            then(dve.tensor_tensor(m3, biased.rearrange("p i (g j) -> p (i g) j", g=8), gm[0], ALU.mult))
            then(dve.tensor_tensor(m3, m3, gm[1], ALU.add))
            for i in range(NTT):
                then(dve.max(etop[:, i, :], masked[:, i, :]))
                then(dve.max_index(eidx_u[:, i, :], etop[:, i, :], masked[:, i, :]))
            then(dve.tensor_copy(eidx, eidx_u))
            then(dve.tensor_tensor(onehot, iota64.unsqueeze(1).unsqueeze(1).broadcast_to([128, NTT, TOPK, NE]),
                                   eidx[:, :, 0:TOPK].unsqueeze(3).broadcast_to([128, NTT, TOPK, NE]), ALU.is_equal))
            then(dve.tensor_reduce(chosen, onehot.rearrange("p i k e -> p i e k"), AX.X, ALU.add))
            done(dve.tensor_tensor(chosen, chosen, valid[:, 0:NTT].unsqueeze(2).broadcast_to([128, NTT, NE]), ALU.mult), chosen_done)
            then(dve.tensor_tensor(prod, onehot, score.unsqueeze(2).broadcast_to([128, NTT, TOPK, NE]), ALU.mult))
            then(dve.tensor_reduce(wsel, prod, AX.X, ALU.add))
            then(dve.tensor_reduce(wsum[:, 0:NTT], wsel, AX.X, ALU.add))
            then(dve.reciprocal(wsum[:, 0:NTT], wsum[:, 0:NTT]))
            then(dve.tensor_scalar(wsum[:, 0:NTT], wsum[:, 0:NTT], ROUTED_SCALE, None, ALU.mult))
            then(dve.tensor_tensor(wsel, wsel, wsum[:, 0:NTT].unsqueeze(2).broadcast_to([128, NTT, TOPK]), ALU.mult))
            dve.wait_ge(rk_ps, 4 + 2)
            then(dve.tensor_copy(count, psum[:, 1, 0:NE]))
            then(dve.tensor_copy(rank, psum[:, 0, 0:NTT * NE].rearrange("p (i e) -> p i e", i=NTT)))
            then(dve.tensor_scalar(ntile, count, 0.0, None, ALU.is_gt))
            for m in range(1, 5):
                then(dve.scalar_tensor_tensor(ntile, count, 128.0 * m, ntile, ALU.is_gt, ALU.add))
            then(dve.tensor_tensor_scan(tile_end, ones[:, 0:NE], ntile, 0.0, ALU.mult, ALU.add))
            then(dve.tensor_tensor(tile_start, tile_end, ntile, ALU.subtract))
            then(dve.tensor_scalar(cmp_i, tile_end, iota_p, None, ALU.is_le))
            then(dve.tensor_reduce(item_f, cmp_i, AX.X, ALU.add))
            then(dve.tensor_scalar(item_i, item_f, float(NE - 1), None, ALU.min))
            then(dve.tensor_scalar(cmp_i, iota64, 2.0, tile_end[:, NE - 1:NE], ALU.mult, ALU.is_lt))
            then(dve.tensor_reduce(item_f, cmp_i, AX.X, ALU.add))
            done(dve.tensor_scalar(n_i, item_f, -2.0, 2.0, ALU.add, ALU.mult), tables)
            then(dve.tensor_scalar(over, rank, 128.0, None, ALU.is_ge))
            for m in range(2, 5):
                then(dve.scalar_tensor_tensor(over, rank, 128.0 * m, over, ALU.is_ge, ALU.add))
            then(dve.scalar_tensor_tensor(rank, over, -128.0, rank, ALU.mult, ALU.add))
            then(dve.tensor_tensor(over, over, tile_start.unsqueeze(1).broadcast_to([128, NTT, NE]), ALU.add))
            then(dve.scalar_tensor_tensor(rank, rank, float(MAXI), over, ALU.mult, ALU.add))
            then(dve.tensor_tensor(prod, onehot, rank.unsqueeze(2).broadcast_to([128, NTT, TOPK, NE]), ALU.mult))
            then(dve.tensor_reduce(posf, prod, AX.X, ALU.add))
            then(dve.tensor_scalar(valid, valid, -1.0, -float(NOWHERE), ALU.add, ALU.mult))
            done(dve.tensor_tensor(pos_i.rearrange("p (i k) -> p i k", i=NTT), posf,
                                   valid[:, 0:NTT].unsqueeze(2).broadcast_to([128, NTT, TOPK]), ALU.add), slots_in)

            def turned_rows(item, u, first=False):
                dve.wait_ge(tr1, 22 + item + 1)
                if not first:
                    dve.wait_ge(sg_ps, 5 + item - 1)
                dve.tensor_copy(hgT[u][:, 4:8, :].rearrange("p c s -> p (c s)"), psum[:, 1, :]).then_inc(hx_v, 1)

            def product(item, u, first=False):
                dve.wait_ge(sg_act, 5 + item + 1)
                if not first:
                    dve.wait_ge(sg_tr, 5 + item - 1)
                dve.tensor_tensor(acte[u], sile[u], psum[:, 2 + u, EFF:2 * EFF], ALU.mult).then_inc(sg_mul, 1)

            def expert_out(item, u, stored=None):
                dve.wait_ge(sd_ps, 5 + item + 1)
                if stored is not None:
                    dve.wait_ge(y_stored[u], stored)
                dve.tensor_copy(ye[u][:, 512:], psum[:, 6, :]).then_inc(sd_out, 1)

            rest = n_items(dve)
            turned_rows(0, 0, True)
            product(0, 0, True)
            turned_rows(1, 1, True)
            product(1, 1, True)
            turned_rows(2, 0)
            expert_out(0, 0)
            product(2, 0)
            turned_rows(3, 1)
            expert_out(1, 1)
            product(3, 1)
            turned_rows(4, 0)
            expert_out(2, 0, 16)
            with dve.Fori(4, rest + 4, 2) as i:
                product(i, 0)
                turned_rows(i + 1, 1)
                expert_out(i - 1, 1, (i - 2) * 8)
                product(i + 1, 1)
                turned_rows(i + 2, 0)
                expert_out(i, 0, i * 8)
            expert_out(rest + 3, 1, (rest + 2) * 8)
            dve.wait_ge(x_landed, 176 + 16 * (NB + 2))
            for i in range(NTT):
                r, kind = tile_rows(i), i // NTP
                acc, x = h2[0:r, i, :], x1[0:r, i, :]
                dve.wait_ge(yk_landed[i % 2], 16 * (i // 2 + 1))
                for k in range(TOPK):
                    ins = dve.scalar_tensor_tensor(acc, ykb[i % 2][0:r, k, :], wsel[0:r, i, k:k + 1], acc, ALU.mult, ALU.add)
                    if k < TOPK - 1:
                        then(ins)
                done(ins, yr_done)
                then(dve.tensor_tensor(acc, acc, g2b[0:r, kind, :], ALU.mult))
                done(dve.tensor_tensor(x, x, acc, ALU.add), x1_done)
                dve.wait_ge(sq1, 10 + i + 1)
                dve.tensor_scalar(rstd[0:r, i:i + 1], ss[0:r, i:i + 1], 1.0 / D, EPS, ALU.mult, ALU.add).then_inc(ms1, 1)
                dve.wait_ge(sqrt1, 2 + i + 1)
                then(dve.reciprocal(rstd[0:r, i:i + 1], rstd[0:r, i:i + 1]))
                dve.scalar_tensor_tensor(x, x, rstd[0:r, i:i + 1], nfb[0:r], ALU.mult, ALU.mult).then_inc(h_ready, 1)

        @block.tensor
        def _(pe):
            def landed(n):
                pe.wait_ge(w_landed[n % 3], 16 * (n // 3 + 1) + (16 if n >= 26 else 0))
                return wring[n % 3]

            pe.wait_ge(c_ready, 1)
            for j in range(12):
                w = landed(j)
                if j >= 2:
                    pe.wait_ge(ada_out, j - 1)
                for c in range(DC):
                    ins = pe.matmul(psum[0:NB + 1, j % 2, :], cT[:, :, c], w[:, c, :], start=(c == 0), stop=(c == DC - 1))
                ins.then_inc(ada_ps, 1)
            pe.wait_ge(pool_const, 1)
            for i in range(NTT + 1):
                T = tile_rows(i) if i < NTT else NB
                if i < NTT:
                    pe.wait_ge(h_ready, i + 1)
                if i >= 2:
                    pe.wait_ge(ev1, 2 * (i - 1))
                for c in range(DC):
                    src = x_all[0:T, i, c::DC] if i < NTT else sstate[:, c::DC]
                    ins = pe.transpose(psum[:, 2 + 2 * (i % 2) + c // 4, T * (c % 4):T * (c % 4) + T], src, ident[0:T, 0:T])
                    if c % 4 == 3:
                        ins.then_inc(tr1, 1)
            pe.wait_ge(ev1, 2 * (NTT + 1))
            pe.wait_ge(ada_out, 12)

            def project(m, w, M, banks):
                for c in range(DC):
                    pe.matmul(psum[0:M, banks[0], :], w[:, c, :], hT[:, c, 0:NP_], start=(c == 0), stop=(c == DC - 1))
                    ins = pe.matmul(psum[0:M, banks[1], 0:NCOL - NP_], w[:, c, :], hT[:, c, NP_:],
                                    start=(c == 0), stop=(c == DC - 1))
                return ins

            m = 0
            for j in range(6):
                w = landed(12 + j)
                a, b = in_cols[j]
                for k in range((b - a) // 128):
                    if m >= 3:
                        pe.wait_ge(pj_out, m - 2)
                    project(m, w[:, :, 128 * k:128 * k + 128], 128, (2 * (m % 3), 2 * (m % 3) + 1)).then_inc(pj_ps, 1)
                    m += 1
            w = landed(18)
            for i in range(NTT):
                r = tile_rows(i)
                if i >= 2:
                    pe.wait_ge(v_out, i - 1)
                for c in range(DC):
                    ins = pe.matmul(psum[0:r, 6 + i % 2, :], hT[:, c, 128 * i:128 * i + r], w[:, c, :], start=(c == 0), stop=(c == DC - 1))
                ins.then_inc(v_ps, 1)
            w = landed(19)
            pe.wait_ge(pj_out, RCH + 2 * NPAIR)
            project(0, w[:, :, 0:H], H, (0, 1)).then_inc(v_ps, 1)
            pe.wait_ge(lf_done, 1)
            for i in range(NTT):
                r = tile_rows(i)
                if i >= 2:
                    pe.wait_ge(kt_out, i - 1)
                    pe.wait_ge(lf_out, i - 1)
                for p in range(NPAIR):
                    ins = pe.transpose(psum[0:r, 2 + i % 2, 128 * p:128 * p + 128], kT[:, p, 128 * i:128 * i + r], ident)
                ins.then_inc(kt_ps, 1)
                pe.transpose(psum[0:r, 4 + i % 2, 0:H], fT[0:H, 128 * i:128 * i + r], ident[0:H, 0:H]).then_inc(lf_ps, 1)

            pe.wait_ge(lora_in, 2)
            pe.wait_ge(lora_landed, 48)
            pe.wait_ge(kt_out, NTT)
            pe.wait_ge(lf_out, NTT)
            pe.wait_ge(f_act, 1)
            for q in range(3 * NPAIR):
                p, k = q // 3, q % 3
                if q >= 3:
                    pe.wait_ge(lora_out, q - 2)
                lhs = (lora_wa[0:64], lora_wa[64:128], lora_g)[k][:, 128 * p:128 * p + 128]
                rhs = (PM[0:64, 12, :], PM[64:128, 12, :], PM[:, 13, :])[k]
                pe.matmul(psum[:, 2 * (q % 3), :], lhs, rhs[:, 0:NP_], start=True, stop=True)
                pe.matmul(psum[:, 2 * (q % 3) + 1, 0:NSM], lhs, rhs[:, NP_:], start=True, stop=True).then_inc(lora_ps, 1)
            pe.wait_ge(lora_out, 3 * NPAIR)
            for p in range(NPAIR):
                pe.wait_ge(kk_sq, p + 1)
                if p >= 2:
                    pe.wait_ge(kk_norm, p - 1)
                pe.matmul(psum[:, 2 * (p % 2), :], blk64, BV[:, p, 0:NP_], start=True, stop=True)
                pe.matmul(psum[:, 2 * (p % 2) + 1, 0:NSM], blk64, BV[:, p, NP_:], start=True, stop=True).then_inc(kk_n2, 1)
            for p in range(NPAIR):
                pe.wait_ge(rk_in, p + 1)
                if p >= 2:
                    pe.wait_ge(prep_done, p - 1)
                pe.matmul(psum[:, 4 + 2 * (p % 2), :], blk64, BV[:, p, 0:NP_], start=True, stop=True)
                pe.matmul(psum[:, 5 + 2 * (p % 2), 0:NSM], blk64, BV[:, p, NP_:], start=True, stop=True).then_inc(rk_ps, 1)
            pe.wait_ge(prep_done, NPAIR)
            pe.wait_ge(kk_norm, NPAIR)
            for i in range(NTT):
                T = tile_rows(i)
                cols = slice(128 * i, 128 * i + T)
                if i > 0:
                    pe.wait_ge(t_add, lv(i - 1, levels(i - 1) - 1, 1))
                for p in range(NPAIR):
                    if i > 0 or p >= 2:
                        pe.wait_ge(tm_out, 4 * i + p - 1)
                    for k, src in enumerate((vT, khat, AA)):
                        ins = pe.transpose(psum[0:T, p % 2, 128 * k:128 * k + 128], src[:, p, cols], ident)
                    ins.then_inc(tm_ps, 1)
                if i > 0:
                    pe.wait_ge(r_out, i)
                    pe.wait_ge(u_out, i)
                for h in range(H):
                    p, sl = h // 2, slice(64 * (h % 2), 64 * (h % 2) + 64)
                    if i > 0 or h >= 2:
                        pe.wait_ge(at_out, 8 * i + h - 1)
                    for k, (a, b) in enumerate(((AA, KK), (AA, rho), (khat, KK), (khat, rho))):
                        ins = pe.matmul(psum[0:T, 2 + h % 2, 128 * k:128 * k + T], a[sl, p, cols], b[sl, p, cols],
                                        start=True, stop=True)
                    ins.then_inc(at_ps, 1)
                if i > 0:
                    pe.wait_ge(y_out, i)
                    pe.wait_ge(s_out, i)
                pe.wait_ge(tm_out, 4 * i + 4)
                for m in range(levels(i)):
                    for g in range(2):
                        pe.wait_ge(ml_done, lv(i, m, g))
                        if m > 0:
                            pe.wait_ge(t_add, lv(i, m - 1, g))
                        for k in range(4):
                            ins = pe.matmul(psum[0:T, 4 + g, 128 * k:128 * k + T], ML[g][0:T, k, 0:T],
                                            TI[4 * g + k][0:T, 0, 0:T] if m else ident[0:T, 0:T], start=True, stop=True)
                        ins.then_inc(p_ps, 1)
                    for g in range(2):
                        if m == 0:
                            continue
                        pe.wait_ge(p_out, lvp(i, m, g))
                        for k in range(4):
                            T0, Tt = TI[4 * g + k][0:T, 0, 0:T], TI[4 * g + k][0:T, 1, 0:T]
                            b0 = (6, 0)[g]
                            if m < levels(i) - 1:
                                o0 = 256 * (k % 2)
                                pe.matmul(psum[0:T, b0 + k // 2, o0:o0 + T], Tt, TP[g][0:T, k, 0:T], start=True, stop=True)
                                ins = pe.matmul(psum[0:T, b0 + k // 2, o0 + 128:o0 + 128 + T], TP[g][0:T, k, 0:T], Tt,
                                                start=True, stop=True)
                            else:
                                ins = pe.matmul(psum[0:T, b0, 128 * k:128 * k + T], TP[g][0:T, k, 0:T], Tt, start=True, stop=True)
                        ins.then_inc(dt_ps, 1)
                if i == NTP:
                    continue
                pe.wait_ge(s0_ready, i + 1)
                pe.wait_ge(at_out, 8 * i + 8)
                for h in range(H):
                    p, sl = h // 2, slice(64 * (h % 2), 64 * (h % 2) + 64)
                    dst = psum[:, (2, 6)[h % 2], 64 * p:64 * p + 64]
                    pe.matmul(dst, KK[sl, p, cols], S0[sl, p, :], start=True, stop=False)
                    ins = pe.matmul(dst, AT[:, h, 256:384], TM[:, p, 0, sl], start=False, stop=True)
                ins.then_inc(r_ps, 1)
                pe.wait_ge(r_out, i + 1)
                pe.wait_ge(t_add, lv(i, 6, 1))
                for h in range(H):
                    ins = pe.matmul(psum[:, 3, 64 * h:64 * h + 64], TI[h][:, 1, :], Rb[:, h, :], start=True, stop=True)
                ins.then_inc(u_ps, 1)
                pe.wait_ge(u_out, i + 1)
                for h in range(H):
                    p, sl = h // 2, slice(64 * (h % 2), 64 * (h % 2) + 64)
                    dst = psum[sl, 4, 128 * p:128 * p + 128]
                    pe.matmul(dst, S0[sl, p, :], rho[sl, p, cols], start=True, stop=False)
                    pe.matmul(dst, TM[:, p, 0, sl], AT[:, h, 384:512], start=False, stop=False)
                    ins = pe.matmul(dst, Ub[:, h, :], AT[:, h, 128:256], start=False, stop=True)
                ins.then_inc(y_ps, 1)
                for h in range(H):
                    p, sl = h // 2, slice(64 * (h % 2), 64 * (h % 2) + 64)
                    dst = psum[sl, 5, 64 * p:64 * p + 64]
                    pe.matmul(dst, TM[:, p, 1, sl], TM[:, p, 0, sl], start=True, stop=False)
                    ins = pe.matmul(dst, TM[:, p, 2, sl], Ub[:, h, :], start=False, stop=True)
                ins.then_inc(s_ps, 1)
            N = NSM
            pe.wait_ge(lora_landed, 48 + 16 * NPAIR * NB)
            pe.wait_ge(t_add, lv(NTP, 2, 1))
            pe.wait_ge(at_out, 8 * NTT)
            for p in range(NPAIR):
                if p >= 2:
                    pe.wait_ge(st_out, p - 1)
                for b in range(NB):
                    ins = pe.transpose(psum[:, p % 2, 64 * b:64 * b + 64], state_rows(p, b), ident[0:HD, 0:HD])
                ins.then_inc(st_ps, 1)
            pe.wait_ge(st_out, NPAIR)
            for p in range(NPAIR):
                for b in range(NB):
                    for e in range(2):
                        sl, c0 = slice(64 * e, 64 * e + 64), NP_ + NS * b
                        st = rho[sl, p, 64 * b:64 * b + 64]
                        for bank, src in ((2, KK), (3, rho)):
                            ins = pe.matmul(psum[sl, bank, 64 * p + NS * b:64 * p + NS * b + NS], st, src[sl, p, c0:c0 + NS],
                                            start=True, stop=True)
            ins.then_inc(ro_ps, 1)
            pe.wait_ge(ro_out, 2)
            for p in range(NPAIR):
                ins = pe.transpose(psum[0:N, 4, 128 * p:128 * p + 128], ro_sb[:, 0, 64 * p:64 * p + 64], ident)
            ins.then_inc(ro_ps, 1)
            for h in range(H):
                p, sl = h // 2, slice(64 * (h % 2), 64 * (h % 2) + 64)
                ins = pe.matmul(psum[0:N, 5, 64 * h:64 * h + 64], AT[0:N, h, 256:256 + N], TM[0:N, p, 0, sl], start=True, stop=True)
            ins.then_inc(ro_ps, 1)
            pe.wait_ge(r_out_s, 1)
            for h in range(H):
                ins = pe.matmul(psum[0:N, 3, 64 * h:64 * h + 64], TI[h][0:N, 1, 0:N], Rb[0:N, h, :], start=True, stop=True)
            ins.then_inc(u_ps, 1)
            pe.wait_ge(u_out, NTP + 1)
            for h in range(H):
                p, sl = h // 2, slice(64 * (h % 2), 64 * (h % 2) + 64)
                dst = psum[sl, 6, N * p:N * p + N]
                pe.matmul(dst, TM[0:N, p, 0, sl], AT[0:N, h, 384:384 + N], start=True, stop=False)
                ins = pe.matmul(dst, Ub[0:N, h, :], AT[0:N, h, 128:128 + N], start=False, stop=True)
            ins.then_inc(y_ps, 1)
            for h in range(H):
                p, sl = h // 2, slice(64 * (h % 2), 64 * (h % 2) + 64)
                pe.wait_ge(x_ready, h + 1)
                if h >= 4:
                    pe.wait_ge(x_out, p - 1)
                xv, xu = khat[0:N, 2 * (h % 2), 0:512], khat[0:N, 2 * (h % 2) + 1, 0:512]
                pe.matmul(psum[sl, p % 2, :], TM[0:N, p, 1, sl], xv, start=True, stop=False)
                pe.matmul(psum[sl, p % 2, :], TM[0:N, p, 2, sl], xu, start=False, stop=True).then_inc(x_ps, 1)
            pe.wait_ge(y_out, NTP + 1)
            pe.wait_ge(s_out, NTP)
            for q in range(1 + 2 * NPAIR):
                if q >= 2:
                    pe.wait_ge(w_out_, q - 1)
                if q > 0:
                    pe.wait_ge(x_out, (q - 1) // 2 + 1)
                for k in range(4):
                    p = (q - 1) // 2
                    b = 4 * ((q - 1) % 2) + k
                    src = Sst[:, k, :] if q == 0 else rho[:, p, 64 * b:64 * b + 64]
                    ins = pe.transpose(psum[0:HD, 6 + q % 2, 128 * k:128 * k + 128], src, ident)
                ins.then_inc(w_ps, 1)

            pe.wait_ge(w_out_, 1 + 2 * NPAIR)
            pe.wait_ge(x_out, NPAIR)
            for p in range(NPAIR):
                if p >= 2:
                    pe.wait_ge(ln_in, p - 1)
                pe.matmul(psum[:, 2 * (p % 2), :], blk64, YT[:, p, 0:NP_], start=True, stop=True)
                pe.matmul(psum[:, 2 * (p % 2) + 1, 0:NSM], blk64, YT[:, p, NP_:], start=True, stop=True).then_inc(ln_mu, 1)
            for p in range(NPAIR):
                pe.wait_ge(ln_sq, p + 1)
                if p >= 2:
                    pe.wait_ge(ln_sd, p - 1)
                pe.matmul(psum[:, 4 + 2 * (p % 2), :], blk64, khat[:, p, 0:NP_], start=True, stop=True)
                pe.matmul(psum[:, 5 + 2 * (p % 2), 0:NSM], blk64, khat[:, p, NP_:], start=True, stop=True).then_inc(ln_var, 1)
            pe.wait_ge(ln_sd, NPAIR)
            pe.wait_ge(ln_in, NPAIR)
            pe.wait_ge(lf_done, 1 + 1)

            def scores(j):
                qt, h = j // H, j % H
                p, sl, kw = h // 2, slice(64 * (h % 2), 64 * (h % 2) + 64), 128 * (qt + 1)
                if j >= 2:
                    pe.wait_ge(at_ex, j - 1)
                dst = psum[:, j % 2, :]
                pe.matmul(dst[:, 0:kw], qT[sl, p, 128 * qt:128 * qt + 128], kT[sl, p, 0:kw], start=True, stop=False)
                pe.matmul(dst[:, 0:kw], ident[:, h:h + 1].broadcast_to([128, 128]), cum[:, 0:kw], start=False, stop=False)
                pe.matmul(dst[:, kw - 128:kw], ident, low_neg, start=False, stop=True).then_inc(at_sc, 1)

            def outputs(j):
                qt, h = j // H, j % H
                p, sl = h // 2, slice(64 * (h % 2), 64 * (h % 2) + 64)
                pe.wait_ge(at_pt, j + 1)
                if j >= 4:
                    pe.wait_ge(at_oe, j // 2 - 1)
                for k in range(qt + 1):
                    ins = pe.matmul(psum[sl, 4 + (j // 2) % 2, 0:128], vtok[:, k, 64 * h:64 * h + 64],
                                    PTb[j % 2][:, 128 * k:128 * k + 128], start=(k == 0), stop=(k == qt))
                ins.then_inc(at_o, 1)

            scores(0)
            for j in range(NTP * H):
                if j + 1 < NTP * H:
                    scores(j + 1)
                pe.wait_ge(at_pn, j + 1)
                if j >= 2:
                    pe.wait_ge(at_pt, j - 1)
                for k in range(j // H + 1):
                    ins = pe.transpose(psum[:, 2 + j % 2, 128 * k:128 * k + 128], Pb[j % 2][:, 128 * k:128 * k + 128], ident)
                ins.then_inc(at_tp, 1)
                if j >= 1:
                    outputs(j - 1)
            outputs(NTP * H - 1)
            pe.wait_ge(lf_done, 2 + 1)
            pe.matmul(psum[:, 7, 0:H], lower16, sum_off[:, 0:H], start=True, stop=True).then_inc(rev_ps, 1)
            pe.wait_ge(rev_landed, 16)
            pe.wait_ge(lf_done, 4 + 1)
            pe.wait_ge(at_oe, NTP * H // 2)
            pe.wait_ge(at_pt, NTP * H)

            def turn_keys(j):
                q, p = j // 4, j % 4
                if p == 0:
                    pe.wait_ge(k_landed[q % 2], 64 * (q // 2 + 1))
                if j >= 2:
                    pe.wait_ge(kte[j % 2], j // 2)
                for k in range(4):
                    ins = pe.transpose(psum[:, j % 2, 128 * k:128 * k + 128], kpage[q % 2][:, k, 128 * p:128 * p + 128], ident)
                ins.then_inc(kt_tr, 1)

            def sample_scores(b):
                for j in range(16 * b, 16 * b + 16):
                    q, p = j // 4, j % 4
                    if j % 16 == 0:
                        turn_keys(j)
                    if j % 16 < 15:
                        turn_keys(j + 1)
                    dst = psum[0:64, 2 + q % 2, :]
                    if p == 0:
                        if q >= 2:
                            pe.wait_ge(sc_out, q - 1)
                        pe.matmul(dst, head_rows[0:64, b].rearrange("p a b -> p (a b)"), revT[:, 512 * (q % 4):512 * (q % 4) + 512],
                                  start=True, stop=False)
                    pe.wait_ge(kte[j % 2], j // 2 + 1)
                    pe.matmul(dst, qblk[:, 256 * b + 64 * p:256 * b + 64 * p + 64], KTb[j % 2], start=False,
                              stop=(p == 3)).then_inc(kq_mm, 1)
                if b >= 1:
                    pe.wait_ge(nw_out, b)
                dst = psum[0:64, 4, 0:64]
                for p in range(NPAIR):
                    pe.matmul(dst, qblk[:, 256 * b + 64 * p:256 * b + 64 * p + 64], kT[:, p, NP_:], start=(p == 0), stop=False)
                pe.matmul(dst, head8.rearrange("p a b -> p (a b)"), cum[:, NP_:], start=False, stop=False)
                pe.matmul(dst, ident[0:64, 0:64], neg_new[0:64, b, :], start=False, stop=True).then_inc(nw_ps, 1)

            def turn_output(b):
                pe.wait_ge(at_oe, 16 + b + 1)
                for p in range(NPAIR):
                    ins = pe.transpose(psum[:, 7, 64 * p:64 * p + 64], Osb[:, 128 * p:128 * p + 128], ident[0:64, 0:64])
                ins.then_inc(ot_ps, 1)

            for b in range(NB + 1):
                if b < NB:
                    sample_scores(b)
                if b >= 2:
                    turn_output(b - 2)
                if b == 0:
                    continue
                a = b - 1
                pe.wait_ge(at_ex, 32 + a + 1)
                for m in range(3):
                    n = 3 * a + m
                    if n >= 2:
                        pe.wait_ge(at_pt, 32 + n - 1)
                    for k in range(8 if m < 2 else 1):
                        c0 = 128 * (8 * m + k)
                        w = 128 if m < 2 else 64
                        ins = pe.transpose(psum[0:w, 5 + n % 2, 64 * k:64 * k + 64], Ssb[a % 2][:, c0:c0 + w], ident[0:64, 0:64])
                    ins.then_inc(at_tp, 1)
                if a >= 1:
                    pe.wait_ge(yf_out, a)
                pe.wait_ge(at_pt, 32 + 3 * a + 3)
                for g in range(4):
                    q = 4 * a + g
                    pe.wait_ge(v_landed[q % 2], 64 * (q // 2 + 1))
                    for k in range(4):
                        ins = pe.matmul(psum[0:64, 7, :], PTs[a % 2][:, 4 * g + k, :], vpage[q % 2][:, k, :], start=(g + k == 0), stop=False)
                    ins.then_inc(vq_mm, 1)
                pe.matmul(psum[0:64, 7, :], PTs[a % 2][0:64, 16, :], vtok[0:64, NTP, :], start=False, stop=True).then_inc(at_o, 1)
            turn_output(NB - 1)
            pe.wait_ge(yf_out, NB)
            pe.wait_ge(nw_out, NB)
            pe.wait_ge(sc_out, 4 * NB)
            pe.wait_ge(br_landed, 32)
            for m in range(DC):
                wr, wf = landed(20 + 2 * (m // 4)), landed(21 + 2 * (m // 4))
                c = slice(128 * (m % 4), 128 * (m % 4) + 128)
                for k, (w, col, src, n) in enumerate(((wr, c, hT, DC), (w_brr, slice(128 * m, 128 * m + 128), YT, NPAIR),
                                                      (wf, c, hT, DC), (w_brf, slice(128 * m, 128 * m + 128), yfT, NPAIR))):
                    j = 4 * m + k
                    b0 = 2 * (j % 4)
                    if m >= 1:
                        pe.wait_ge(mg_sg, 2 * (m - 1) + k // 2 + 1)
                        if k % 2 == 1:
                            pe.wait_ge(mg_out, m)
                    for a in range(n):
                        pe.matmul(psum[:, b0, :], w[:, a, col], src[:, a, 0:NP_], start=(a == 0), stop=(a == n - 1))
                        ins = pe.matmul(psum[:, b0 + 1, 0:NSM], w[:, a, col], src[:, a, NP_:NT], start=(a == 0), stop=(a == n - 1))
                    ins.then_inc(mg_ps, 1)
            pe.wait_ge(mg_out, DC)
            for half in range(2):
                w = landed(24 + half)
                for i in range(NTT):
                    r, q = tile_rows(i), NTT * half + i
                    if q >= 4:
                        pe.wait_ge(x1_done, q - 3)
                    for a in range(DC):
                        ins = pe.matmul(psum[0:r, q % 4, :], mergedT[:, a, 128 * i:128 * i + r], w[:, a, :], start=(a == 0), stop=(a == DC - 1))
                    ins.then_inc(xo_ps, 1)
            pe.wait_ge(x1_done, 2 * NTT)
            for i in range(NTT):
                T = tile_rows(i)
                pe.wait_ge(h_ready, 5 + i + 1)
                if i >= 2:
                    pe.wait_ge(ev1, 12 + 2 * (i - 1))
                for c in range(DC):
                    ins = pe.transpose(psum[:, 2 * (i % 2) + c // 4, T * (c % 4):T * (c % 4) + T], h2[0:T, i, c::DC], ident[0:T, 0:T])
                    if c % 4 == 3:
                        ins.then_inc(tr1, 1)
            pe.wait_ge(ev1, 12 + 2 * NTT)
            w, wd = landed(26).rearrange("p c n -> p (c n)"), landed(27).rearrange("p c n -> p (c n)")
            for i in range(NTT):
                T = tile_rows(i)
                if i >= 2:
                    pe.wait_ge(f_act, 2 + i - 1)
                for c in range(DC):
                    ins = pe.matmul(psum[0:T, 6 + i % 2, 0:NE], hT[:, c, 128 * i:128 * i + T], wd[:, 2048 + NE * c:2048 + NE * c + NE],
                                    start=(c == 0), stop=(c == DC - 1))
                ins.then_inc(lg_ps, 1)
            pe.wait_ge(f_act, 2 + NTT)
            for i in range(NTT):
                T = tile_rows(i)
                if i >= 2:
                    pe.wait_ge(sg_mul, i - 1)
                for k in range(2):
                    for c in range(DC):
                        ins = pe.matmul(psum[0:T, 4 + i % 2, EFF * k:EFF * k + EFF], hT[:, c, 128 * i:128 * i + T],
                                        w[:, 2048 * k + EFF * c:2048 * k + EFF * c + EFF], start=(c == 0), stop=(c == DC - 1))
                ins.then_inc(sg_ps, 1)
                pe.wait_ge(sg_mul, i + 1)
                if i >= 1:
                    pe.wait_ge(sg_at, i)
                for c in range(2):
                    ins = pe.transpose(psum[:, 6, T * c:T * c + T], act_s[i % 2][0:T, c::2], ident[0:T, 0:T])
                ins.then_inc(sg_tr, 1)
                pe.wait_ge(sg_at, i + 1)
                if i >= 2:
                    pe.wait_ge(sd_out, i - 1)
                for half in range(2):
                    for c in range(2):
                        ins = pe.matmul(psum[0:T, half + 2 * (i % 2), :], actT_s[i % 2][:, c, 0:T],
                                        wd[:, D * c + 512 * half:D * c + 512 * half + 512], start=(c == 0), stop=(c == 1))
                ins.then_inc(sd_ps, 1)

            pe.wait_ge(sd_out, NTT)
            pe.wait_ge(chosen_done, 1)
            for i in range(NTT):
                dst = psum[:, 0, NE * i:NE * i + NE]
                for j in range(i):
                    pe.matmul(dst, ones, chosen[:, j, :], start=(j == 0), stop=False)
                ins = pe.matmul(dst, up_strict, chosen[:, i, :], start=(i == 0), stop=True)
            ins.then_inc(rk_ps, 1)
            for i in range(NTT):
                ins = pe.matmul(psum[:, 1, 0:NE], ones, chosen[:, i, :], start=(i == 0), stop=(i == NTT - 1))
            ins.then_inc(rk_ps, 1)

            def turn_rows(item, u, landed, first=False):
                pe.wait_ge(hg_landed[u], landed)
                if not first:
                    pe.wait_ge(ev1, 22 + item)
                    pe.wait_ge(hx_v, item)
                for c in range(DC):
                    ins = pe.transpose(psum[:, c // 4, 128 * (c % 4):128 * (c % 4) + 128], hg[u][:, c::DC], ident)
                ins.then_inc(tr1, 1)

            def gate_up(item, u, landed, first=False):
                pe.wait_ge(ev1, 22 + item + 1)
                pe.wait_ge(hx_v, item + 1)
                pe.wait_ge(gu_landed[u], landed)
                if not first:
                    pe.wait_ge(sg_mul, 5 + item - 1)
                for k in range(2):
                    for c in range(DC):
                        ins = pe.matmul(psum[:, 2 + u, EFF * k:EFF * k + EFF], hgT[u][:, c, :], wgu[u][:, k, c, :],
                                        start=(c == 0), stop=(c == DC - 1))
                ins.then_inc(sg_ps, 1)

            def turn_act(item, u, first=False):
                pe.wait_ge(sg_mul, 5 + item + 1)
                if not first:
                    pe.wait_ge(sg_at, 5 + item)
                for c in range(2):
                    ins = pe.transpose(psum[:, 4, 128 * c:128 * c + 128], acte[u][:, c::2], ident)
                ins.then_inc(sg_tr, 1)

            def down(item, u, landed, first=False):
                pe.wait_ge(sg_at, 5 + item + 1)
                pe.wait_ge(dn_landed[u], landed)
                if not first:
                    pe.wait_ge(y_a, item)
                    pe.wait_ge(sd_out, 5 + item)
                for half in range(2):
                    for c in range(2):
                        ins = pe.matmul(psum[:, 5 + half, :], acteT[u][:, c, :], wdn[u][:, c, 512 * half:512 * half + 512],
                                        start=(c == 0), stop=(c == 1))
                ins.then_inc(sd_ps, 1)

            rest = n_items(pe)
            pe.wait_ge(slots_in, 1)
            turn_rows(0, 0, 16, True)
            gate_up(0, 0, 32, True)
            turn_rows(1, 1, 16)
            gate_up(1, 1, 32, True)
            turn_act(0, 0, True)
            turn_rows(2, 0, 32)
            down(0, 0, 16, True)
            with pe.Fori(2, rest + 4, 2) as i:
                gate_up(i, 0, i * 16 + 32)
                turn_act(i - 1, 1)
                turn_rows(i + 1, 1, i * 8 + 16)
                down(i - 1, 1, i * 8)
                gate_up(i + 1, 1, i * 16 + 32)
                turn_act(i, 0)
                turn_rows(i + 2, 0, i * 8 + 32)
                down(i, 0, i * 8 + 16)
            turn_act(rest + 3, 1)
            down(rest + 3, 1, (rest + 4) * 8)


def kernel(**inputs):
    import numpy as _np
    import concourse.bacc as _bacc
    from concourse import mybir as _mybir
    from concourse.bass_utils import run_bass_kernel_spmd as _run

    nc = _bacc.Bacc("TRN2", target_bir_lowering=False, num_devices=1)
    arrays, ins, outs = {}, {}, {}
    for name in INS:
        a = _np.ascontiguousarray(inputs[name])
        arrays[f"in_{name}"] = a
        ins[name] = nc.dram_tensor(f"in_{name}", a.shape, _mybir.dt.from_np(a.dtype), kind="ExternalInput").ap()
    for name, shape in OUTS:
        outs[name] = nc.dram_tensor(f"out_{name}", shape, _mybir.dt.float32, kind="ExternalOutput").ap()
    build(nc, ins, outs)
    r = _run(nc, [arrays], core_ids=[0])
    return tuple(r.results[0][f"out_{name}"] for name, _ in OUTS)
```
